# Optimizing a Trainium2 kernel written in Bass

```python
import jax, jax.numpy as jnp
from jax import lax
import numpy as np

D_MODEL = 1024
BATCH = 1
SEQ = 1024
DEPTH = 1

HEAD_DIM = 64
N_Q_HEADS = 8
N_KV_HEADS = 2
ATTN_WIDTH = N_Q_HEADS * HEAD_DIM
KV_WIDTH = N_KV_HEADS * HEAD_DIM
CONV_WIDTH = D_MODEL - ATTN_WIDTH
MIX_WIDTH = ATTN_WIDTH + CONV_WIDTH
CONV_KERNEL = 31
WINDOW = 128
BLOCK = 128
ROPE_THETA = 10000.0
EPS = 1e-6
IN_WIDTH = ATTN_WIDTH + 2 * KV_WIDTH + ATTN_WIDTH + 2 * CONV_WIDTH + CONV_WIDTH

kernel_name = "hybrid_swa_sink_conformer_adaln"

def _rms_norm(t, w):
    tf = t.astype(jnp.float32)
    y = tf * lax.rsqrt(jnp.mean(tf * tf, axis=-1, keepdims=True) + EPS)
    return (y * w.astype(jnp.float32)).astype(t.dtype)

def _layer_norm(t, w, b):
    tf = t.astype(jnp.float32)
    mu = jnp.mean(tf, axis=-1, keepdims=True)
    var = jnp.mean(jnp.square(tf - mu), axis=-1, keepdims=True)
    y = (tf - mu) * lax.rsqrt(var + EPS)
    return (y * w.astype(jnp.float32) + b.astype(jnp.float32)).astype(t.dtype)

def _rope_tables(seq_len):
    inv = ROPE_THETA ** (-jnp.arange(0, HEAD_DIM, 2, dtype=jnp.float32) / HEAD_DIM)
    ang = jnp.arange(seq_len, dtype=jnp.float32)[:, None] * inv[None, :]
    return jnp.cos(ang), jnp.sin(ang)

def _apply_rope(t, cos, sin):
    tf = t.astype(jnp.float32)
    t1, t2 = jnp.split(tf, 2, axis=-1)
    c_, s_ = cos[None, :, None, :], sin[None, :, None, :]
    return jnp.concatenate([t1 * c_ - t2 * s_, t2 * c_ + t1 * s_], axis=-1).astype(t.dtype)

def _sliding_window_sink_attention(q, k, v, sinks):
    B, S, _, dh = q.shape
    nb = S // BLOCK
    G = N_Q_HEADS // N_KV_HEADS
    qb = q.reshape(B, nb, BLOCK, N_KV_HEADS, G, dh)

    def band(t):
        tb = t.reshape(B, nb, BLOCK, N_KV_HEADS, dh)
        prev = jnp.concatenate([jnp.zeros_like(tb[:, :1]), tb[:, :-1]], axis=1)
        return jnp.concatenate([prev, tb], axis=2)

    kb, vb = band(k), band(v)
    s = jnp.einsum('bnqhgd,bnkhd->bnhgqk', qb, kb,
                   preferred_element_type=jnp.float32) * (dh ** -0.5)
    qi = jnp.arange(BLOCK)[:, None]
    kj = jnp.arange(2 * BLOCK)[None, :]
    dist = qi + BLOCK - kj
    local = (dist >= 0) & (dist < WINDOW)
    exists = (jnp.arange(nb)[:, None, None] > 0) | (kj[None] >= BLOCK)
    mask = local[None] & exists
    s = jnp.where(mask[None, :, None, None], s, -jnp.inf)
    sink = sinks.astype(jnp.float32).reshape(1, 1, N_KV_HEADS, G, 1, 1)
    m = jnp.maximum(jnp.max(s, axis=-1, keepdims=True), sink)
    p = jnp.exp(s - m)
    p = p / (jnp.sum(p, axis=-1, keepdims=True) + jnp.exp(sink - m))
    o = jnp.einsum('bnhgqk,bnkhd->bnqhgd', p.astype(v.dtype), vb)
    return o.reshape(B, S, N_Q_HEADS * dh)

def _conformer_conv(u, conv_w, conv_b, ln_w, ln_b):
    a, g = jnp.split(u, 2, axis=-1)
    z = a * jax.nn.sigmoid(g)
    z = lax.conv_general_dilated(
        z, conv_w[:, None, :], window_strides=(1,),
        padding=[(CONV_KERNEL - 1, 0)],
        dimension_numbers=('NWC', 'WIO', 'NWC'),
        feature_group_count=CONV_WIDTH) + conv_b
    z = _layer_norm(z, ln_w, ln_b)
    return jax.nn.silu(z)

def setup_inputs(seed: int = 0) -> dict:
    key = jax.random.key(seed)
    ks = jax.random.split(key, 16)
    f32 = jnp.float32
    n = lambda k, shape, s: jax.random.normal(k, shape, f32) * s
    return {
        "x": n(ks[0], (BATCH, SEQ, D_MODEL), 1.0),
        "c": n(ks[1], (BATCH, D_MODEL), 1.0),
        "w_ada": n(ks[2], (DEPTH, D_MODEL, 3 * D_MODEL), 0.5 * D_MODEL ** -0.5),
        "b_ada": n(ks[3], (DEPTH, 3 * D_MODEL), 0.02),
        "norm_w": 1.0 + n(ks[4], (DEPTH, D_MODEL), 0.02),
        "w_in": n(ks[5], (DEPTH, D_MODEL, IN_WIDTH), D_MODEL ** -0.5),
        "q_norm_w": 1.0 + n(ks[6], (DEPTH, HEAD_DIM), 0.02),
        "k_norm_w": 1.0 + n(ks[7], (DEPTH, HEAD_DIM), 0.02),
        "sinks": n(ks[8], (DEPTH, N_Q_HEADS), 0.5),
        "conv_w": n(ks[9], (DEPTH, CONV_KERNEL, CONV_WIDTH), CONV_KERNEL ** -0.5),
        "conv_b": n(ks[10], (DEPTH, CONV_WIDTH), 0.02),
        "ln_w": 1.0 + n(ks[11], (DEPTH, CONV_WIDTH), 0.02),
        "ln_b": n(ks[12], (DEPTH, CONV_WIDTH), 0.02),
        "w_out": n(ks[13], (DEPTH, MIX_WIDTH, D_MODEL), MIX_WIDTH ** -0.5),
    }

def reference(x, c, w_ada, b_ada, norm_w, w_in, q_norm_w, k_norm_w, sinks,
              conv_w, conv_b, ln_w, ln_b, w_out):
    B, S, _ = x.shape
    cos, sin = _rope_tables(S)
    c_act = jax.nn.silu(c)
    splits = (ATTN_WIDTH,
              ATTN_WIDTH + KV_WIDTH,
              ATTN_WIDTH + 2 * KV_WIDTH,
              2 * ATTN_WIDTH + 2 * KV_WIDTH,
              2 * ATTN_WIDTH + 2 * KV_WIDTH + 2 * CONV_WIDTH)
    for l in range(DEPTH):
        shift, scale, gate = jnp.split(c_act @ w_ada[l] + b_ada[l], 3, axis=-1)
        h = _rms_norm(x, norm_w[l]) * (1.0 + scale[:, None, :]) + shift[:, None, :]
        proj = h @ w_in[l]
        q, k, v, gate_a, u, gate_b = jnp.split(proj, splits, axis=-1)
        q = q.reshape(B, S, N_Q_HEADS, HEAD_DIM)
        k = k.reshape(B, S, N_KV_HEADS, HEAD_DIM)
        v = v.reshape(B, S, N_KV_HEADS, HEAD_DIM)
        q = _apply_rope(_rms_norm(q, q_norm_w[l]), cos, sin)
        k = _apply_rope(_rms_norm(k, k_norm_w[l]), cos, sin)
        y_a = _sliding_window_sink_attention(q, k, v, sinks[l]) * jax.nn.silu(gate_a)
        y_b = _conformer_conv(u, conv_w[l], conv_b[l], ln_w[l], ln_b[l]) * jax.nn.silu(gate_b)
        y = jnp.concatenate([y_a, y_b], axis=-1) @ w_out[l]
        x = x + gate[:, None, :] * y
    return x


_drawn_inputs = setup_inputs


def setup_inputs(seed=0):
    import zlib

    import numpy as np

    out = dict(_drawn_inputs(seed))
    spreads = {}
    factors = {'b_ada': 7.04,
     'norm_w': 8.0,
     'q_norm_w': 8.0,
     'k_norm_w': 8.0,
     'sinks': 64.0,
     'conv_b': 26.486,
     'ln_w': 39.335,
     'ln_b': 40.595}
    for name, (base, spread) in spreads.items():
        noise = np.random.default_rng([zlib.crc32(name.encode()), seed]).standard_normal(out[name].shape)
        drawn = base * np.exp(spread * noise) if base else spread * noise
        out[name] = __import__('jax').numpy.asarray(drawn.astype(out[name].dtype))
    for name, factor in factors.items():
        out[name] = (out[name] * factor).astype(out[name].dtype)
    return out
```

```python
from contextlib import ExitStack

import numpy as np

import concourse.bass as bass
from concourse import mybir

F32 = mybir.dt.float32
F32R = mybir.dt.float32r
U8 = mybir.dt.uint8
ALU = mybir.AluOpType
ACT = mybir.ActivationFunctionType
AX = mybir.AxisListType

P = 128
D = 1024
S = 1024
HALF = 512
KT = D // P
NT = S // P
DH = 64
NH = 8
NKV = 2
GRP = NH // NKV
TAPS = 31
PAD = TAPS - 1
ZW = S + 32
NCT = 4
EPS = 1e-6
FILL = -1.0e38
U = 256
Q0, K0, GA0, A0, G0, GB0 = 0, 512, 768, 1280, 1792, 2304


def build(nc, x, c, w_ada, b_ada, norm_w, w_in, q_norm_w, k_norm_w, sinks,
          conv_w, conv_b, ln_w, ln_b, w_out, rope_rows, out):
    base = 16512

    def at(name, shape, dtype, offset):
        return nc.alloc_sbuf_tensor_at(name, [P] + shape, dtype, offset=base + offset)

    H_AT, W_AT, RAW_AT, XG_AT, C_AT, S_AT = 0, 65536, 131072, 143360, 176128, 201216
    Z_AT = W_AT
    h = at("h", [2, KT, S], F32R, H_AT)
    wts = at("wts", [4, 2, KT, U], F32R, W_AT)
    sel0 = at("sel0", [NH, P], F32, Z_AT)
    pcur = at("pcur", [GRP, P], F32, Z_AT + 4096)
    pprev = at("pprev", [GRP, P], F32, Z_AT + 6144)
    qk = at("qk", [10 * DH], F32, Z_AT + 8192)
    rot1 = at("rot1", [10 * DH], F32, Z_AT + 10752)
    rot2 = at("rot2", [10 * DH], F32, Z_AT + 13312)
    vrows = at("vrows", [P], F32, Z_AT)
    cwrows = at("cwrows", [512], F32, Z_AT + 512)
    h32 = at("h32", [2, HALF], F32, Z_AT + 2560)
    junk = at("junk", [D], F32, Z_AT + 6656)
    ada_acc = at("ada_acc", [2, 2, 2 * P], F32, Z_AT + 10752)
    gdiag = at("gdiag", [NT, P], F32, Z_AT + 8192)
    raw = at("raw", [3, 1024], F32, RAW_AT)
    xs = at("xs", [NT, D], F32, XG_AT)
    att = at("att", [NCT, S], F32, XG_AT)
    gb = at("gb", [NCT, S], F32, XG_AT + 16384)
    gacc = at("gacc", [D], F32, XG_AT + 16384)
    sel1 = at("sel1", [NH, P], F32, XG_AT + 16384 + 12288)
    xr = at("xr", [NT, D], F32, XG_AT)
    z = at("z", [NCT, ZW], F32, C_AT)
    cacc = at("cacc", [2, S], F32, C_AT + 4 * 4 * ZW)
    slab = at("slab", [3, KT, 2, P], F32, C_AT)
    lnbuf = at("lnbuf", [2, ZW], F32, C_AT + 2 * 4 * ZW)
    v = at("v", [5, P], F32, S_AT)
    qT = at("qT", [GRP, P], F32, S_AT + 2560)
    kT = at("kT", [2, P], F32, S_AT + 4608)
    ropr = at("ropr", [P], F32, S_AT + 5632)
    tab = at("tab", [2, 2, NKV, DH], F32, S_AT + 6144)
    gbc = at("gbc", [D], F32, S_AT)
    obuf = at("obuf", [2, HALF], F32, S_AT + 4096)
    spot = [S_AT + 8192]

    def small(name, shape, dtype=F32):
        t = at(name, shape, dtype, spot[0])
        n = int(np.prod(shape)) * (1 if dtype == U8 else 4)
        spot[0] += -(-n // 32) * 32
        return t

    ident = small("ident", [P])
    ones = small("ones", [P])
    later = small("later", [P], U8)
    cols = small("cols", [52])
    cw = small("cw", [NCT, TAPS])
    wqk = small("wqk", [NKV, DH])
    snk = small("snk", [NH])
    nsnk = small("nsnk", [NH])
    mhalf = small("mhalf", [10])
    cact = small("cact", [KT])
    tiny = small("tiny", [12])
    ssx = small("ssx", [NT])
    rsx = small("rsx", [NT])
    ssq = small("ssq", [10])
    rsq = small("rsq", [10])
    modA = small("modA", [KT])
    modB = small("modB", [KT])
    bs1 = small("bs1", [KT])
    gcol = small("gcol", [KT])
    nmx = small("nmx", [2, NH])
    sdiff = small("sdiff", [NH])
    esink = small("esink", [NH])
    psum_p = small("psum_p", [NH])
    rden = small("rden", [NH])
    lnc = small("lnc", [4, NCT])
    assert spot[0] <= 229344 - base, spot[0]
    C_C, C_NW, C_SH, C_SC, C_GT, C_CB, C_LW, C_LB = 0, 8, 16, 24, 32, 40, 44, 48

    with ExitStack() as ctx:
        def psum(name, shape):
            return ctx.enter_context(nc.psum_tensor(name, [P] + shape, F32))

        def sem(name):
            return ctx.enter_context(nc.semaphore(name))

        pm = psum("pm", [3, HALF])
        ps = psum("ps", [2, HALF])
        tr = psum("tr", [2, HALF])
        pv = psum("pv", [HALF])

        s_vec, s_cw, s_bc = sem("s_vec"), sem("s_cw"), sem("s_bc")
        s_x = [sem(f"s_x{t}") for t in range(NT)]
        s_slab = [sem(f"s_slab{i}") for i in range(3)]
        s_raw = [sem(f"s_raw{i}") for i in range(3)]
        s_rope = sem("s_rope")
        s_xr = [sem(f"s_xr{t}") for t in range(NT)]
        s_out = sem("s_out")
        g_const, g_rsx, g_lo, g_tab = sem("g_const"), sem("g_rsx"), sem("g_lo"), sem("g_tab")
        g_sd, g_rs, g_mask, g_rope = sem("g_sd"), sem("g_rs"), sem("g_mask"), sem("g_rope")
        g_den, g_blk0, g_ylo, g_fin, g_link = sem("g_den"), sem("g_blk0"), sem("g_ylo"), sem("g_fin"), sem("g_link")
        g_s01, g_rstd = sem("g_s01"), sem("g_rstd")
        p_rows, p_xT, p_ada, p_main = sem("p_rows"), sem("p_xT"), sem("p_ada"), sem("p_main")
        p_gcol, p_gbc, p_T, p_S, p_PT, p_PV = sem("p_gcol"), sem("p_gbc"), sem("p_T"), sem("p_S"), sem("p_PT"), sem("p_PV")
        p_mean, p_var, p_bc, p_out = sem("p_mean"), sem("p_var"), sem("p_bc"), sem("p_out")
        a_cols, a_ssx, a_h32, a_hi, a_tanh = sem("a_cols"), sem("a_ssx"), sem("a_h32"), sem("a_hi"), sem("a_tanh")
        a_v, a_pt, a_exp, a_qT, a_sel = sem("a_v"), sem("a_pt"), sem("a_exp"), sem("a_qT"), sem("a_sel")
        a_pn, a_att, a_yhi, a_gbc, a_sq, a_ty = sem("a_pn"), sem("a_att"), sem("a_yhi"), sem("a_gbc"), sem("a_sq"), sem("a_ty")
        a_link = sem("a_link")
        d_cact, d_xn, d_ada, d_ab, d_hhi, d_hlo = sem("d_cact"), sem("d_xn"), sem("d_ada"), sem("d_ab"), sem("d_hhi"), sem("d_hlo")
        d_glu, d_conv, d_gp, d_gcol, d_ss, d_qn = sem("d_glu"), sem("d_conv"), sem("d_gp"), sem("d_gcol"), sem("d_ss"), sem("d_qn")
        d_cp, d_nmx, d_rden, d_gate, d_ya = sem("d_cp"), sem("d_nmx"), sem("d_rden"), sem("d_gate"), sem("d_ya")
        d_gdiag, d_s23, d_dm, d_var, d_ldiag, d_e, d_v, d_yb, d_o, d_link = (
            sem("d_gdiag"), sem("d_s23"), sem("d_dm"), sem("d_var"), sem("d_ldiag"), sem("d_e"), sem("d_v"),
            sem("d_yb"), sem("d_o"), sem("d_link"))

        units = [(w_in, A0), (w_in, G0), (w_in, G0 + U), (w_in, A0 + U), (w_in, Q0), (w_in, Q0 + U), (w_in, K0),
                 (w_in, GB0), (w_in, GB0 + U), (w_in, GA0), (w_in, GA0 + U),
                 (w_out, U), (w_out, 0), (w_out, 2 * U), (w_out, 3 * U)]
        slots = [1, 2, 3, 1, 2, 3, 1, 2, 3, 1, 2, 3, 0, 1, 2]
        used = [8, 8, 14, 16, 31, 31, 32, 36, 40, 44, 48]
        free = [0, 0, 0, used[0], used[1], used[2], used[3], used[4], used[5], used[6], used[7],
                used[8], 0, used[9], used[10]]
        pieces = [(0, 0), (1, 0), (0, 1), (1, 1)] + [(u, p) for u in range(2, len(units)) for p in range(2)]
        raws = [("w", i) for i in range(10)] + [("g", i) for i in range(KT)] + [("w", i) for i in range(10, len(pieces))]
        raw_at = {key: r for r, key in enumerate(raws)}

        def transfers(u, p):
            src, c0 = units[u]
            if src is w_in:
                return 4 if GA0 <= c0 < A0 else 1
            return 2 if p == 0 else 1

        raw_due = []
        total = [0, 0, 0]
        for r, (kind, i) in enumerate(raws):
            total[r % 3] += 16 * (transfers(*pieces[i]) if kind == "w" else 1)
            raw_due.append(total[r % 3])

        def split_done(u):
            return max(i for i, (w, _) in enumerate(pieces) if w == u) + 1

        def whalf(i):
            u, p = pieces[i]
            return slots[u], slice(4 * p, 4 * p + 4)

        block = ctx.enter_context(nc.Block())

        @block.sync
        def _(sp):
            k0 = 0
            for vec, n in ((c, 8), (norm_w, 8), (b_ada, 24), (conv_b, 4), (ln_w, 4), (ln_b, 4)):
                sp.dma_start(vrows[k0:k0 + n, :], vec[0].rearrange("(r p) -> r p", p=P)).then_inc(s_vec, 16)
                k0 += n
            for t in range(4):
                sp.dma_start(xs[:, t, :], x[0, t * P:(t + 1) * P, :]).then_inc(s_x[t], 16)

            def load_raw(r):
                kind, i = raws[r]
                if r >= 3:
                    was, n = raws[r - 3]
                    sp.wait_ge(g_lo if was == "w" else d_gp, n + 1)
                dst = raw[:, r % 3, :]
                if kind == "g":
                    sp.dma_start(dst, w_ada[0, i * P:(i + 1) * P, 2 * D:3 * D]).then_inc(s_raw[r % 3], 16)
                    return
                u, p = pieces[i]
                src, c0 = units[u]
                if src is w_out and p == 0:
                    for g in range(NKV):
                        sp.dma_start(raw[g * DH:(g + 1) * DH, r % 3, :].rearrange("p (k n) -> p k n", k=4),
                                     src[0, g * 256:(g + 1) * 256, c0:c0 + U].rearrange("(k p) n -> p k n", p=DH)
                                     ).then_inc(s_raw[r % 3], 16)
                    return
                if transfers(u, p) == 4:
                    for j in range(2):
                        for g in range(NKV):
                            first = GA0 + (4 * g + 2 * ((c0 - GA0) // U) + j) * DH
                            sp.dma_start(dst.rearrange("p (k j g d) -> p k j g d", k=4, j=2, g=NKV)[:, :, j, g, :],
                                         src[0, p * 512:(p + 1) * 512, first:first + DH].rearrange("(k p) d -> p k d", p=P)
                                         ).then_inc(s_raw[r % 3], 16)
                    return
                sp.dma_start(dst.rearrange("p (k n) -> p k n", k=4),
                             src[0, p * 512:(p + 1) * 512, c0:c0 + U].rearrange("(k p) n -> p k n", p=P)
                             ).then_inc(s_raw[r % 3], 16)

            def load_slab(k):
                if k >= 3:
                    sp.wait_ge(p_ada, k - 2)
                for part in range(2):
                    sp.dma_start(slab[:, k % 3, :, part, :],
                                 w_ada[0, :, part * D + k * P:part * D + (k + 1) * P].rearrange("(t p) n -> p t n", p=P)
                                 ).then_inc(s_slab[k % 3], 16)

            load_raw(0)
            load_raw(1)
            load_slab(0)
            sp.dma_start(cwrows[0:TAPS, :], conv_w[0]).then_inc(s_cw, 16)
            load_slab(1)
            load_raw(2)
            load_slab(2)
            load_raw(3)
            sp.dma_start(wqk[:, 0, :], q_norm_w.to_broadcast([P, DH])).then_inc(s_bc, 16)
            sp.dma_start(wqk[:, 1, :], k_norm_w.to_broadcast([P, DH])).then_inc(s_bc, 16)
            sp.dma_start(snk[:, :], sinks.to_broadcast([P, NH])).then_inc(s_bc, 16)
            for k in range(3, KT):
                load_slab(k)
            for t in range(4, NT):
                sp.dma_start(xs[:, t, :], x[0, t * P:(t + 1) * P, :]).then_inc(s_x[t], 16)

            def load_rope(t):
                if t:
                    sp.wait_ge(g_tab, t)
                sp.dma_start(ropr[:, :], rope_rows[t * P:(t + 1) * P, :]).then_inc(s_rope, 16)

            r = 4
            while raws[r] != ("w", 12):
                load_raw(r)
                r += 1
            load_rope(0)
            load_raw(r)
            load_raw(r + 1)
            r += 2
            for t in range(1, NT):
                load_rope(t)
            while r < len(raws):
                load_raw(r)
                r += 1
                if raws[r - 1] == ("w", 27):
                    for t in range(4):
                        sp.wait_ge(g_ylo, 4)
                        sp.dma_start(xr[:, t, :], x[0, t * P:(t + 1) * P, :]).then_inc(s_xr[t], 16)
            for t in range(4, NT):
                sp.wait_ge(g_ylo, t + 1)
                sp.dma_start(xr[:, t, :], x[0, t * P:(t + 1) * P, :]).then_inc(s_xr[t], 16)
            for i in range(2 * NT):
                sp.wait_ge(g_fin, i + 1)
                t, n = i % NT, i // NT
                sp.dma_start(out[0, t * P:(t + 1) * P, n * HALF:(n + 1) * HALF],
                             xr[:, t, n * HALF:(n + 1) * HALF]).then_inc(s_out, 16)
            sp.wait_ge(s_out, 16 * 2 * NT)

        @block.gpsimd
        def _(gp):
            linked = [0]

            def link(ins):
                linked[0] += 1
                ins.then_inc(g_link, 1)
                gp.wait_ge(g_link, linked[0])

            gp.memset(ones[:, :], 1.0).then_inc(g_const, 1)
            gp.memset(mhalf[:, :], -0.5).then_inc(g_const, 1)
            gp.wait_ge(g_const, 2)
            gp.affine_select(out=ident[:, :], in_=ones[:, :], compare_op=ALU.is_equal, fill=0.0,
                             base=0, pattern=[[-1, P]], channel_multiplier=1).then_inc(g_const, 1)
            link(gp.affine_select(out=junk[:, 0:P], in_=ones[:, :], compare_op=ALU.is_gt, fill=0.0,
                                  base=0, pattern=[[1, P]], channel_multiplier=-1))
            gp.tensor_copy(later[:, :], junk[:, 0:P]).then_inc(g_const, 1)

            def rms_x(half):
                gp.wait_ge(a_ssx, 4 * half + 4)
                sl = slice(4 * half, 4 * half + 4)
                link(gp.tensor_scalar(tiny[:, 0:4], ssx[:, sl], 1.0 / D, EPS, ALU.mult, ALU.add))
                gp.tensor_tensor(rsx[:, sl], tiny[:, 0:4], mhalf[:, 0:4], ALU.pow).then_inc(g_rsx, 1)

            def w_lo(i):
                gp.wait_ge(a_hi, i + 1)
                slot, ks = whalf(i)
                gp.tensor_tensor(wts[:, slot, 1, ks, :],
                                 raw[:, raw_at["w", i] % 3, :].rearrange("p (k n) -> p k n", k=4),
                                 wts[:, slot, 0, ks, :].bitcast(F32), ALU.subtract).then_inc(g_lo, 1)

            rms_x(0)
            for i in range(4):
                w_lo(i)
            gp.wait_ge(s_bc, 48)
            link(gp.tensor_scalar(wqk[:, 0, :], wqk[:, 0, :], DH ** -0.5, None, ALU.mult))
            link(gp.tensor_scalar(nsnk[:, :], snk[:, :], -1.0, None, ALU.mult))
            rms_x(1)
            for i in range(4, 10):
                w_lo(i)

            def tables(t):
                gp.wait_ge(s_rope, 16 * (t + 1))
                if t >= 2:
                    gp.wait_ge(g_rope, t - 1)
                cc = ropr[:, 0:DH].unsqueeze(1).to_broadcast([P, NKV, DH])
                gp.tensor_tensor(tab[:, t % 2, 0, :, :], cc, wqk[:, :, :], ALU.mult)
                for lo, other in ((0, 32), (32, 0)):
                    ss = ropr[:, DH + lo:DH + lo + 32].unsqueeze(1).to_broadcast([P, NKV, 32])
                    last = gp.tensor_tensor(tab[:, t % 2, 1, :, lo:lo + 32], ss, wqk[:, :, other:other + 32], ALU.mult)
                last.then_inc(g_tab, 1)

            def rms_qk(t):
                gp.wait_ge(d_ss, t + 1)
                if t:
                    gp.wait_ge(d_qn, t)
                link(gp.tensor_scalar(tiny[:, 0:10], ssq[:, :], 1.0 / DH, EPS, ALU.mult, ALU.add))
                gp.tensor_tensor(rsq[:, :], tiny[:, 0:10], mhalf[:, :], ALU.pow).then_inc(g_rs, 1)

            def rope(t):
                gp.wait_ge(d_qn, t + 1)
                gp.wait_ge(g_tab, t + 1)
                if t:
                    gp.wait_ge(p_T, t)
                q, k = slice(0, 512), slice(512, 640)
                for i, part, grp, n in ((0, q, NKV, GRP), (1, k, 1, NKV)):
                    src = qk[:, part].rearrange("p (g j d) -> p g j d", g=grp, d=DH)
                    r1 = rot1[:, part].rearrange("p (j g d) -> p g j d", g=grp, d=DH)
                    r2 = rot2[:, part].rearrange("p (j g d) -> p g j d", g=grp, d=DH)
                    co = tab[:, t % 2, 0, i, :].unsqueeze(1).unsqueeze(1).to_broadcast([P, grp, n, DH])
                    gp.tensor_tensor(r1, src, co, ALU.mult)
                    for lo, other in ((0, 32), (32, 0)):
                        si = tab[:, t % 2, 1, i, lo:lo + 32].unsqueeze(1).unsqueeze(1).to_broadcast([P, grp, n, 32])
                        last = gp.tensor_tensor(r2[:, :, :, lo:lo + 32], src[:, :, :, other:other + 32], si, ALU.mult)
                link(last)
                gp.tensor_tensor(rot1[:, :], rot1[:, :], rot2[:, :], ALU.add).then_inc(g_rope, 1)

            def masks(b, g):
                gp.wait_ge(a_pt, 2 * b + g + 1)
                if b:
                    gp.affine_select(out=pprev[:, :, :], in_=pcur[:, :, :], compare_op=ALU.is_gt, fill=0.0,
                                     base=0, pattern=[[0, GRP], [-1, P]], channel_multiplier=1).then_inc(g_link, 1)
                    linked[0] += 1
                    gp.wait_ge(g_link, linked[0])
                gp.affine_select(out=pcur[:, :, :], in_=pcur[:, :, :], compare_op=ALU.is_ge, fill=0.0,
                                 base=0, pattern=[[0, GRP], [1, P]], channel_multiplier=-1).then_inc(g_mask, 1)

            def sink_diff(b):
                gp.wait_ge(d_nmx, b + 1)
                if b:
                    gp.wait_ge(a_exp, b)
                gp.tensor_tensor(sdiff[:, :].rearrange("p (jj g jh) -> p jj g jh", jj=2, g=NKV),
                                 nmx[:, b % 2, :].rearrange("p (jj g jh) -> p jj g jh", jj=2, g=NKV),
                                 snk[:, :].rearrange("p (g jj jh) -> p jj g jh", g=NKV, jj=2), ALU.add).then_inc(g_sd, 1)

            def denominator(b):
                gp.wait_ge(a_exp, b + 1)
                gp.tensor_tensor(psum_p[:, :], psum_p[:, :], esink[:, :], ALU.add).then_inc(g_den, 1)

            tables(0)
            for i in range(10, 14):
                w_lo(i)
            for n in range(12):
                b2, b3, b4, t = n - 2, n - 3, n - 4, n - 1
                if 0 <= b3 < NT:
                    sink_diff(b3)
                if 0 <= t < NT:
                    rms_qk(t)
                if 0 <= b4 < NT:
                    masks(b4, 0)
                if 0 <= b4 < NT:
                    masks(b4, 1)
                if 0 <= b3 < NT:
                    denominator(b3)
                if 0 <= t < NT:
                    rope(t)
                if b2 == 0:
                    gp.wait_ge(a_sel, 2)
                    gp.affine_select(out=sel0[:, :, :], in_=sel0[:, :, :], compare_op=ALU.is_ge, fill=FILL,
                                     base=0, pattern=[[0, NH], [-1, P]], channel_multiplier=1).then_inc(g_blk0, 1)
                if n + 1 < NT:
                    tables(n + 1)
                if n == 7:
                    for i in range(14, 18):
                        w_lo(i)
                if n == 8:
                    w_lo(18)
                    w_lo(19)
                if n == 10:
                    w_lo(20)
                    w_lo(21)
            for i in range(22, 26):
                w_lo(i)

            def y_lo(k, src):
                gp.wait_ge(a_yhi, k + 1)
                gp.tensor_tensor(h[:, 1, k, :], src, h[:, 0, k, :].bitcast(F32), ALU.subtract).then_inc(g_ylo, 1)

            gp.wait_ge(d_conv, 4 * TAPS)
            gp.tensor_tensor(lnbuf[:, 0, 0:S], cacc[:, 0, :], cacc[:, 1, :], ALU.add).then_inc(g_s01, 1)
            for j in range(NCT):
                y_lo(j, att[:, j, :])
            for i in range(26, 30):
                w_lo(i)
            gp.wait_ge(d_var, 1)
            link(gp.tensor_scalar(tiny[:, 0:8], ssx[:, :], 1.0 / 512, EPS, ALU.mult, ALU.add))
            gp.tensor_tensor(rsx[:, :], tiny[:, 0:8], mhalf[:, 0:8], ALU.pow).then_inc(g_rstd, 1)
            for i in range(NCT):
                y_lo(NCT + i, gb[:, i, :])

            for i in range(2 * NT):
                gp.wait_ge(d_o, i + 1)
                t, n = i % NT, i // NT
                gp.wait_ge(s_xr[t], 16)
                sl = slice(n * HALF, (n + 1) * HALF)
                gp.tensor_tensor(xr[:, t, sl], xr[:, t, sl], obuf[:, i % 2, :], ALU.add).then_inc(g_fin, 1)

        @block.tensor
        def _(pe):
            pe.wait_ge(g_const, 4)
            pe.wait_ge(s_vec, 96)
            pe.transpose(pv[:, 0:52], vrows[0:52, :], ident[0:52, 0:52]).then_inc(p_rows, 1)

            def x_transposes(idx):
                half, k = idx // KT, idx % KT
                if k == 0:
                    pe.wait_ge(d_xn, 4 * half + 4)
                if idx >= 2:
                    pe.wait_ge(a_h32, idx - 1)
                for t in range(4):
                    last = pe.transpose(tr[:, k % 2, t * P:(t + 1) * P], xs[:, 4 * half + t, k * P:(k + 1) * P], ident[:, :])
                last.then_inc(p_xT, 1)

            def ada_bank(k):
                return pv if k % 2 == 0 else ps[:, 1, :]

            def ada_cols(k):
                if k == 0:
                    pe.wait_ge(d_cact, 1)
                    pe.wait_ge(a_cols, 3)
                if k >= 2:
                    pe.wait_ge(d_ab, 2 * (k - 1))
                pe.wait_ge(s_slab[k % 3], 32 * (k // 3 + 1))
                pe.wait_ge(d_ada, 6 * k + 6)
                for part in range(2):
                    o = ada_bank(k)[:, part:part + 1]
                    for ct in (6, 7):
                        pe.matmul(o, slab[:, k % 3, ct, part, :], cact[:, ct:ct + 1], start=(ct == 6), stop=False)
                    for ch in range(2):
                        last = pe.matmul(o, ada_acc[:, k % 2, ch, part * P:(part + 1) * P], ones[:, 0:1],
                                         start=False, stop=(ch == 1))
                last.then_inc(p_ada, 1)

            def three(out, hi_w, lo_w, hi_x, lo_x, first, last):
                pe.matmul(out, hi_w, hi_x, start=first, stop=False)
                pe.matmul(out, lo_w, hi_x, start=False, stop=False)
                return pe.matmul(out, hi_w, lo_x, start=False, stop=last)

            def channel_step(out, slot, col, half, k):
                sl = slice(half * HALF, (half + 1) * HALF)
                return three(out, wts[:, slot + 1, 0, k, col:col + P], wts[:, slot + 1, 1, k, col:col + P],
                             h[:, 0, k, sl], h[:, 1, k, sl], k == 0, k == KT - 1)

            x_transposes(0)
            pe.wait_ge(s_cw, 16)
            pe.wait_ge(a_cols, 1)
            for i in range(NCT):
                last = pe.transpose(pv[:, 64 + 32 * i:64 + 32 * i + TAPS], cwrows[0:TAPS, i * P:(i + 1) * P],
                                    ident[0:TAPS, 0:TAPS])
            last.then_inc(p_rows, 1)
            ada_cols(0)
            early = [(pm[:, 0, :], 1, 0), (pm[:, 1, :], 1, P), (pm[:, 2, :], 0, 0), (ps[:, 0, :], 0, P)]
            for k in range(KT):
                if k + 1 < KT:
                    x_transposes(k + 1)
                    ada_cols(k + 1)
                pe.wait_ge(d_hlo, k + 1)
                if k % 4 == 0:
                    pe.wait_ge(g_lo, 2 if k == 0 else 4)
                for bank, slot, col in early:
                    last = channel_step(bank, slot, col, 0, k)
                    if k == KT - 1:
                        last.then_inc(p_main, 1)
            for k in range(KT):
                x_transposes(KT + k)

            def channel_tile(out, slot, col, half):
                for k in range(KT):
                    if half == 1:
                        pe.wait_ge(d_hlo, KT + k + 1)
                    last = channel_step(out, slot, col, half, k)
                return last

            pe.wait_ge(d_ab, 16)
            channel_tile(ps[:, 1, :], 1, 0, 1).then_inc(p_main, 1)
            channel_tile(pv[:, :], 0, 0, 1).then_inc(p_main, 1)
            pe.wait_ge(a_tanh, 1)
            channel_tile(pm[:, 0, :], 1, P, 1).then_inc(p_main, 1)
            pe.wait_ge(a_tanh, 2)
            channel_tile(pm[:, 1, :], 0, P, 1).then_inc(p_main, 1)

            def bank(i):
                return pm[:, (i - 6) % 3, :]

            def wait_bank(i):
                j = i - 3
                if j == 5:
                    pe.wait_ge(d_glu, 1)
                elif j == 6:
                    pe.wait_ge(a_tanh, 4)
                elif j == 7:
                    pe.wait_ge(d_glu, 4)
                elif j < 16:
                    pair, part = (j - 8) // 4, (j - 8) % 4
                    if part < 2:
                        pe.wait_ge(a_tanh, 4 + 2 * pair + part + 1)
                    else:
                        pe.wait_ge(d_glu, 4 + 2 * pair + part - 1)
                elif j < 32:
                    pe.wait_ge(d_qn, (j - 16) // 2 + 1)
                else:
                    pe.wait_ge(d_gate, j - 31)

            use = 8
            for pair in range(2):
                for slot in (2, 0):
                    if pair == 0:
                        pe.wait_ge(g_lo, split_done(2 if slot == 2 else 3))
                    for half in range(2):
                        wait_bank(use)
                        for k in range(KT):
                            last = channel_step(bank(use), slot, pair * P, half, k)
                        last.then_inc(p_main, 1)
                        use += 1
            pe.wait_ge(d_gp, KT)
            pe.wait_ge(a_h32, 16)
            for i in range(KT):
                last = pe.matmul(tr[:, 0, i:i + 1], gacc[:, i * P:(i + 1) * P], ones[:, 0:1], start=True, stop=True)
            last.then_inc(p_gcol, 1)

            def transpose_qk(b):
                pe.wait_ge(g_rope, b + 1)
                if b == 0:
                    pe.wait_ge(d_gcol, 1)
                else:
                    pe.wait_ge(a_qT, b)
                if b >= 2:
                    pe.wait_ge(a_pt, 2 * (b - 1))
                for j in range(GRP):
                    pe.transpose(tr[:, 0, j * P:(j + 1) * P], rot1[:, j * P:(j + 1) * P], ident[:, :])
                pe.transpose(tr[:, 1, 0:P], rot1[:, 512:640], ident[:, :]).then_inc(p_T, 1)

            def scores(b, jj):
                pe.wait_ge(a_qT, b + 1)
                if b == 0 and jj == 0:
                    pe.wait_ge(d_glu, 2)
                    pe.wait_ge(a_tanh, 3)
                if 2 * b + jj:
                    pe.wait_ge(a_sel, 2 * b + jj)
                if 2 * (b - 1) + jj > 0:
                    pe.wait_ge(d_cp, 2 * (b - 1) + jj)
                for jh in range(2):
                    for g in range(NKV):
                        lhs = qT[g * DH:(g + 1) * DH, 2 * jj + jh, :]
                        if b:
                            o, rhs = ps[:, g, jh * 256:(jh + 1) * 256], kT[g * DH:(g + 1) * DH, :, :]
                        else:
                            o, rhs = ps[:, g, jh * 256:jh * 256 + P], kT[g * DH:(g + 1) * DH, 0, :]
                        last = pe.matmul(o, lhs, rhs, start=True, stop=True)
                last.then_inc(p_S, 1)

            def transpose_p(b):
                pe.wait_ge(a_pn, b + 1)
                pe.wait_ge(a_qT, min(b + 2, NT))
                if b:
                    pe.wait_ge(a_pt, 2 * b)
                s = sel1 if b % 2 else sel0
                for g in range(NKV):
                    for j in range(GRP):
                        last = pe.transpose(tr[:, g, j * P:(j + 1) * P], s[:, (j // 2) * 4 + g * 2 + j % 2, :], ident[:, :])
                    last.then_inc(p_PT, 1)

            def times_v(b, g):
                pe.wait_ge(g_mask, 2 * b + g + 1)
                pe.wait_ge(a_v, b + 1)
                if b:
                    pe.wait_ge(a_att, b)
                else:
                    pe.wait_ge(d_glu, 3)
                o = pv[g * DH:(g + 1) * DH, :]
                last = pe.matmul(o, v[:, b % 5, g * DH:(g + 1) * DH], pcur[:, :, :], start=True, stop=(b == 0))
                if b:
                    last = pe.matmul(o, v[:, (b - 1) % 5, g * DH:(g + 1) * DH], pprev[:, :, :], start=False, stop=True)
                last.then_inc(p_PV, 1)

            def attention_step(n, s):
                new, old = n - 2, n - 4
                if 0 <= old < NT:
                    if s == 0:
                        transpose_p(old)
                    if s == 6:
                        times_v(old, 0)
                    if s == 15:
                        times_v(old, 1)
                if 0 <= new < NT:
                    if s == 9:
                        transpose_qk(new)
                    if s == 12:
                        scores(new, 0)
                    if s == 15:
                        scores(new, 1)

            pe.wait_ge(g_lo, split_done(5))
            for t in range(NT):
                ts = slice(t * P, (t + 1) * P)
                for part in range(2):
                    i = 16 + 2 * t + part
                    if t == 0 and part == 1:
                        pe.wait_ge(g_lo, split_done(6))
                    for k in range(KT):
                        attention_step(t, part * KT + k)
                        if k == 0:
                            wait_bank(i)
                        if part == 0:
                            o = bank(i).rearrange("p (s n) -> p s n", s=2)
                            w_hi, w_lo = wts[:, 2:4, 0, k, :], wts[:, 2:4, 1, k, :]
                        else:
                            o = bank(i)[:, 0:256]
                            w_hi, w_lo = wts[:, 1, 0, k, :], wts[:, 1, 1, k, :]
                        x_hi, x_lo = h[:, 0, k, ts], h[:, 1, k, ts]
                        pe.matmul(o, x_hi, w_hi, start=(k == 0), stop=False)
                        pe.matmul(o, x_hi, w_lo, start=False, stop=False)
                        last = pe.matmul(o, x_lo, w_hi, start=False, stop=(k == KT - 1))
                    last.then_inc(p_main, 1)

            def gate_row():
                pe.wait_ge(d_gdiag, 1)
                pe.wait_ge(a_pt, 2 * NT)
                for half in range(2):
                    last = pe.matmul(tr[:, half, :], ones[:, :], gdiag[:, 4 * half:4 * half + 4, :], start=True, stop=True)
                last.then_inc(p_gbc, 1)

            for m in range(2 * NCT):
                n = NT + m
                for half in range(2):
                    i = 32 + 2 * m + half
                    for k in range(KT):
                        attention_step(n, half * KT + k)
                        if m == 5 and half == 0 and k == 0:
                            gate_row()
                        if k == 0:
                            wait_bank(i)
                            if half == 0 and m % 2 == 0:
                                pe.wait_ge(g_lo, split_done(7 + m // 2))
                        last = channel_step(bank(i), (1 + m // 2) % 3, (m % 2) * P, half, k)
                    last.then_inc(p_main, 1)

            pe.wait_ge(g_s01, 1)
            pe.wait_ge(d_s23, 1)
            pe.wait_ge(d_cp, 14)
            for half in range(2):
                sl = slice(half * HALF, (half + 1) * HALF)
                for i in range(2):
                    last = pe.matmul(ps[:, half, :], ones[:, :], lnbuf[:, i, sl], start=(i == 0), stop=(i == 1))
            last.then_inc(p_mean, 1)

            obanks = [tr[:, 0, :], tr[:, 1, :], pm[:, 0, :], pm[:, 1, :], pm[:, 2, :]]

            def out_step(i, k):
                t, n = i % NT, i // NT
                ts = slice(t * P, (t + 1) * P)
                o = obanks[i % 5].rearrange("p (s n) -> p s n", s=2)
                w = [wts[:, 0:4:3, part, k, :] if n == 0 else wts[:, 1:3, part, k, :] for part in range(2)]
                pe.matmul(o, h[:, 0, k, ts], w[0], start=(k == 0), stop=False)
                pe.matmul(o, h[:, 0, k, ts], w[1], start=False, stop=False)
                return pe.matmul(o, h[:, 1, k, ts], w[0], start=False, stop=(k == KT - 1))

            pe.wait_ge(g_lo, split_done(12))
            for i in range(5):
                if i == 0:
                    pe.wait_ge(a_gbc, 1)
                elif i >= 2:
                    pe.wait_ge(d_gate, 14 + i - 2)
                for k in range(NCT):
                    if i == 0:
                        pe.wait_ge(g_ylo, k + 1)
                    out_step(i, k)
                if i == 1:
                    for ct in range(NCT):
                        pe.wait_ge(a_sq, ct + 1)
                        if ct == 0:
                            pe.wait_ge(a_att, NT)
                        for t in range(NT):
                            last = pe.matmul(pv[:, t:t + 1], lnbuf[:, ct % 2, t * P:(t + 1) * P], ones[:, 0:1],
                                             start=(ct == 0 and t == 0), stop=(ct == NCT - 1), skip_group_check=True)
                        last.then_inc(p_var, 1)
                if i == 3:
                    pe.wait_ge(d_ldiag, 1)
                    for half in range(2):
                        last = pe.matmul(ps[:, half, :], ones[:, :], lnbuf[:, 0, half * HALF:(half + 1) * HALF],
                                         start=True, stop=True)
                    last.then_inc(p_bc, 1)
            for i in range(2 * NT):
                if i >= 5:
                    pe.wait_ge(d_o, i - 4)
                if i == NT:
                    pe.wait_ge(g_lo, split_done(14))
                for k in range(NCT if i < 5 else 0, KT):
                    if i == 0:
                        pe.wait_ge(g_ylo, k + 1)
                    last = out_step(i, k)
                last.then_inc(p_out, 1)

        @block.scalar
        def _(act):
            linked = [0]

            def link(ins):
                linked[0] += 1
                ins.then_inc(a_link, 1)
                act.wait_ge(a_link, linked[0])

            act.wait_ge(p_rows, 1)
            act.activation(cols[:, :], pv[:, 0:52], ACT.Copy).then_inc(a_cols, 1)
            act.wait_ge(a_cols, 1)
            act.activation(cact[:, :], cols[:, C_C:C_C + KT], ACT.Tanh, scale=0.5).then_inc(a_cols, 1)

            def sum_x(t):
                act.wait_ge(s_x[t], 16)
                if t:
                    act.wait_ge(a_ssx, t)
                act.activation(junk[:, :], xs[:, t, :], ACT.Square, accum_out=ssx[:, t:t + 1]).then_inc(a_ssx, 1)

            def w_hi(i):
                u, _ = pieces[i]
                r = raw_at["w", i]
                act.wait_ge(s_raw[r % 3], raw_due[r])
                if free[u]:
                    act.wait_ge(p_main, free[u])
                slot, ks = whalf(i)
                act.activation(wts[:, slot, 0, ks, :], raw[:, r % 3, :].rearrange("p (k n) -> p k n", k=4),
                               ACT.Copy).then_inc(a_hi, 1)

            def modulate(idx):
                k = idx % KT
                act.wait_ge(p_xT, idx + 1)
                if idx < KT:
                    act.wait_ge(d_ab, 2 * k + 2)
                if idx >= 2:
                    act.wait_ge(d_hlo, idx - 1)
                act.activation(h32[:, idx % 2, :], tr[:, idx % 2, :], ACT.Identity, scale=modA[:, k:k + 1],
                               bias=modB[:, k:k + 1]).then_inc(a_h32, 1)

            act.wait_ge(g_const, 4)
            sum_x(0)
            sum_x(1)
            sum_x(2)
            sum_x(3)
            act.wait_ge(p_rows, 2)
            act.activation(cw[:, :, :], pv[:, 64:192].rearrange("p (i t) -> p i t", t=32)[:, :, 0:TAPS], ACT.Copy,
                           scale=0.5).then_inc(a_cols, 1)
            for i in range(3):
                w_hi(i)
            modulate(0)
            w_hi(3)
            for k in range(1, KT):
                modulate(k)
            for t in range(4, NT):
                sum_x(t)

            def tanh_g(i, half, src, use):
                act.wait_ge(p_main, use + 1)
                act.activation(z[:, i, PAD + half * HALF:PAD + (half + 1) * HALF], src, ACT.Tanh,
                               scale=0.5).then_inc(a_tanh, 1)

            tanh_g(0, 0, pm[:, 0, :], 0)
            tanh_g(1, 0, pm[:, 1, :], 1)
            for idx in range(KT, 2 * KT):
                modulate(idx)
            w_hi(4)
            w_hi(5)
            tanh_g(0, 1, ps[:, 1, :], 4)
            tanh_g(1, 1, pm[:, 0, :], 6)
            for i in range(6, 10):
                w_hi(i)
            for i, use in ((2, 8), (3, 12)):
                for half in range(2):
                    tanh_g(i, half, pm[:, (use + half - 6) % 3, :], use + half)
            for i in range(10, 14):
                w_hi(i)

            def bank(i):
                return pm[:, (i - 6) % 3, :]

            def squares_v(t):
                act.wait_ge(p_main, 16 + 2 * t + 2)
                if t:
                    act.wait_ge(g_rope, t)
                    act.wait_ge(d_ss, t)
                if t >= 5:
                    act.wait_ge(p_PV, 2 * (t - 4) + 2)
                act.activation(rot2[:, 0:512], bank(16 + 2 * t), ACT.Square)
                act.activation(rot2[:, 512:640], bank(17 + 2 * t)[:, 0:P], ACT.Square)
                act.activation(v[:, t % 5, :], bank(17 + 2 * t)[:, P:2 * P], ACT.Copy, scale=0.5).then_inc(a_v, 1)

            def copy_pt(b, g):
                act.wait_ge(p_PT, 2 * b + g + 1)
                if 2 * b + g:
                    act.wait_ge(p_PV, 2 * b + g)
                act.activation(pcur[:, :, :], tr[:, g, :].rearrange("p (j n) -> p j n", j=GRP), ACT.Copy).then_inc(a_pt, 1)

            def exps(b):
                s = sel1 if b % 2 else sel0
                act.wait_ge(d_nmx, b + 1)
                act.wait_ge(g_sd, b + 1)
                if b:
                    act.wait_ge(d_rden, b)
                for i in range(NH):
                    act.activation(s[:, i, :], s[:, i, :], ACT.Exp, bias=nmx[:, b % 2, i:i + 1],
                                   accum_out=psum_p[:, i:i + 1])
                act.activation(esink[:, :], sdiff[:, :], ACT.Exp).then_inc(a_exp, 1)

            def copy_qk(b):
                act.wait_ge(p_T, b + 1)
                if b:
                    act.wait_ge(p_S, 2 * b)
                act.activation(qT[:, :, :], tr[:, 0, :].rearrange("p (j n) -> p j n", j=GRP), ACT.Copy)
                act.activation(kT[:, b % 2, :], tr[:, 1, 0:P], ACT.Copy).then_inc(a_qT, 1)

            def copy_scores(b, jj):
                s = sel1 if b % 2 else sel0
                act.wait_ge(p_S, 2 * b + jj + 1)
                if b >= 2 and jj == 0:
                    act.wait_ge(p_PT, 2 * (b - 2) + 2)
                src = ps[:, :, :].rearrange("p g (j s n) -> p (g j) s n", j=2, s=2)[:, :, b % 2, :]
                act.activation(s[:, 4 * jj:4 * jj + 4, :], src, ACT.Copy).then_inc(a_sel, 1)

            def normalize(b):
                s = sel1 if b % 2 else sel0
                act.wait_ge(d_rden, b + 1)
                for i in range(NH):
                    last = act.activation(s[:, i, :], s[:, i, :], ACT.Copy, scale=rden[:, i:i + 1])
                last.then_inc(a_pn, 1)

            def copy_att(b):
                act.wait_ge(p_PV, 2 * b + 2)
                act.activation(att[:, :, b * P:(b + 1) * P], pv[:, :].rearrange("p (j n) -> p j n", j=GRP),
                               ACT.Copy).then_inc(a_att, 1)

            def tanh_gate(m, half):
                i = 32 + 2 * m + half
                act.wait_ge(p_main, i + 1)
                if m < NCT:
                    if m == 0:
                        act.wait_ge(d_gcol, 1)
                    if m == 3:
                        act.wait_ge(p_PT, 16)
                    dst = gb[:, m, half * HALF:(half + 1) * HALF]
                else:
                    if m > NCT:
                        act.wait_ge(d_ya, 2 * (m - NCT - 1) + half + 1)
                    dst = obuf[:, half, :]
                act.activation(dst, bank(i), ACT.Tanh, scale=0.5).then_inc(a_tanh, 1)

            for n in range(16):
                t, b2, b3, b4 = n - 1, n - 2, n - 3, n - 4
                if n > 8:
                    tanh_gate(n - 9, 0)
                    tanh_gate(n - 9, 1)
                if 0 <= t < NT:
                    squares_v(t)
                if 0 <= b4 < NT:
                    copy_pt(b4, 0)
                if 0 <= b3 < NT:
                    exps(b3)
                if 0 <= b4 < NT:
                    copy_pt(b4, 1)
                if 0 <= b2 < NT:
                    copy_qk(b2)
                    copy_scores(b2, 0)
                if 0 <= b3 < NT:
                    normalize(b3)
                if 0 <= b2 < NT:
                    copy_scores(b2, 1)
                if 0 <= b4 < NT:
                    copy_att(b4)
                if n == 7:
                    for i in range(14, 18):
                        w_hi(i)
                if n == 8:
                    w_hi(18)
                    w_hi(19)
                if n == 10:
                    w_hi(20)
                    w_hi(21)
                if n == 12:
                    w_hi(22)
                    w_hi(23)
                if n == 13:
                    act.wait_ge(p_gbc, 1)
                    act.wait_ge(p_PV, 16)
                    act.activation(gbc[:, :].rearrange("p (a n) -> p a n", a=2), tr[:, :, :], ACT.Copy).then_inc(a_gbc, 1)
                    w_hi(24)
                    w_hi(25)
            tanh_gate(7, 0)
            tanh_gate(7, 1)

            def y_hi(k, src):
                act.activation(h[:, 0, k, :], src, ACT.Copy).then_inc(a_yhi, 1)

            act.wait_ge(p_main, 48)
            for j in range(NCT):
                act.wait_ge(d_ya, 2 * j + 2)
                y_hi(j, att[:, j, :])
            conv_out = [cacc[:, 0, :], cacc[:, 1, :], z[:, 0, 0:S], z[:, 1, 0:S]]
            for ct in range(NCT):
                act.wait_ge(d_dm, ct + 1)
                if ct == 0:
                    act.wait_ge(p_mean, 1)
                if ct >= 2:
                    act.wait_ge(p_var, ct - 1)
                act.activation(lnbuf[:, ct % 2, 0:S], conv_out[ct], ACT.Square).then_inc(a_sq, 1)
            for i in range(26, 30):
                w_hi(i)
            for ct in range(NCT):
                act.wait_ge(d_e, ct + 1)
                if ct >= 1:
                    act.wait_ge(d_yb, ct)
                act.activation(lnbuf[:, 1, 0:S], conv_out[ct], ACT.Tanh, scale=lnc[:, 0, ct:ct + 1],
                               bias=lnc[:, 1, ct:ct + 1]).then_inc(a_ty, 1)
                act.wait_ge(d_yb, ct + 1)
                y_hi(NCT + ct, gb[:, ct, :])

        @block.vector
        def _(dve):
            linked = [0]

            def link(ins):
                linked[0] += 1
                ins.then_inc(d_link, 1)
                dve.wait_ge(d_link, linked[0])

            dve.wait_ge(a_cols, 2)
            link(dve.scalar_tensor_tensor(out=cact[:, :], in0=cact[:, :], scalar=1.0, in1=cols[:, C_C:C_C + KT],
                                          op0=ALU.add, op1=ALU.mult))
            dve.tensor_scalar(cact[:, :], cact[:, :], 0.5, None, ALU.mult).then_inc(d_cact, 1)
            dve.tensor_scalar(bs1[:, :], cols[:, C_SC:C_SC + KT], 1.0, None, ALU.add)
            for i, (c0, f) in enumerate(((C_LW, 0.5), (C_LB, 0.5), (C_LW, 0.25), (C_LB, 0.25))):
                last = dve.tensor_scalar(lnc[:, i, :], cols[:, c0:c0 + NCT], f, None, ALU.mult)
            last.then_inc(d_cact, 1)

            def normalize_x(t):
                dve.tensor_scalar(xs[:, t, :], xs[:, t, :], rsx[:, t:t + 1], None, ALU.mult).then_inc(d_xn, 1)

            def ada_sums(k):
                if k == 0:
                    dve.wait_ge(d_cact, 2)
                dve.wait_ge(s_slab[k % 3], 32 * (k // 3 + 1))
                if k >= 2:
                    dve.wait_ge(p_ada, k - 1)
                for i in range(3):
                    for ch in range(2):
                        ct = 3 * ch + i
                        acc = ada_acc[:, k % 2, ch, :]
                        src = slab[:, k % 3, ct, :, :].rearrange("p a n -> p (a n)")
                        if i == 0:
                            ins = dve.tensor_scalar(acc, src, cact[:, ct:ct + 1], None, ALU.mult)
                        else:
                            dve.wait_ge(d_ada, 6 * k + 2 * i + ch - 1)
                            ins = dve.scalar_tensor_tensor(out=acc, in0=src, scalar=cact[:, ct:ct + 1], in1=acc,
                                                           op0=ALU.mult, op1=ALU.add)
                        ins.then_inc(d_ada, 1)

            def ada_finish(k):
                dve.wait_ge(p_ada, k + 1)
                b = pv if k % 2 == 0 else ps[:, 1, :]
                dve.scalar_tensor_tensor(out=modA[:, k:k + 1], in0=b[:, 1:2], scalar=bs1[:, k:k + 1],
                                         in1=cols[:, C_NW + k:C_NW + k + 1], op0=ALU.add, op1=ALU.mult).then_inc(d_ab, 1)
                dve.tensor_tensor(modB[:, k:k + 1], b[:, 0:1], cols[:, C_SH + k:C_SH + k + 1], ALU.add).then_inc(d_ab, 1)

            def split_h(idx):
                half, k = idx // KT, idx % KT
                sl = slice(half * HALF, (half + 1) * HALF)
                dve.wait_ge(a_h32, idx + 1)
                dve.tensor_copy(h[:, 0, k, sl], h32[:, idx % 2, :]).then_inc(d_hhi, 1)
                dve.wait_ge(d_hhi, idx + 1)
                dve.tensor_tensor(h[:, 1, k, sl], h32[:, idx % 2, :], h[:, 0, k, sl].bitcast(F32),
                                  ALU.subtract).then_inc(d_hlo, 1)

            dve.wait_ge(g_rsx, 1)
            for t in range(4):
                normalize_x(t)
            ada_sums(0)
            ada_finish(0)
            for k in range(KT):
                if k + 1 < KT:
                    ada_sums(k + 1)
                split_h(k)
                if k + 1 < KT:
                    ada_finish(k + 1)
            dve.wait_ge(g_rsx, 2)
            for t in range(4, NT):
                normalize_x(t)
            for idx in range(KT, 2 * KT):
                split_h(idx)
            dve.wait_ge(p_ada, KT)
            dve.memset(z[:, :, 0:PAD], 0.0).then_inc(d_link, 1)
            linked[0] += 1

            def glu(i, half, src, use, n_tanh):
                dve.wait_ge(p_main, use + 1)
                dve.wait_ge(a_tanh, n_tanh)
                sl = slice(PAD + half * HALF, PAD + (half + 1) * HALF)
                dve.scalar_tensor_tensor(out=z[:, i, sl], in0=z[:, i, sl], scalar=1.0, in1=src,
                                         op0=ALU.add, op1=ALU.mult).then_inc(d_glu, 1)

            done = [0]

            def conv(n):
                for s in range(done[0], done[0] + n):
                    g, j = s // TAPS, s % TAPS
                    if j == 0:
                        dve.wait_ge(d_link, linked[0])
                        dve.wait_ge(d_glu, 4 * g + 4)
                        if g == 1:
                            dve.wait_ge(d_conv, 2 * TAPS)
                    for e in range(2):
                        i = 2 * g + e
                        acc = cacc[:, e, :] if g == 0 else z[:, e, 0:S]
                        src = z[:, i, j:j + S]
                        if j == 0:
                            ins = dve.tensor_scalar(acc, src, cw[:, i, 0:1], cols[:, C_CB + i:C_CB + i + 1],
                                                    ALU.mult, ALU.add)
                        else:
                            dve.wait_ge(d_conv, 2 * s + e - 1)
                            ins = dve.scalar_tensor_tensor(out=acc, in0=src, scalar=cw[:, i, j:j + 1], in1=acc,
                                                           op0=ALU.mult, op1=ALU.add)
                        ins.then_inc(d_conv, 1)
                done[0] += n

            dve.wait_ge(a_cols, 3)
            glu(0, 0, pm[:, 2, :], 2, 1)
            glu(1, 0, ps[:, 0, :], 3, 2)
            glu(0, 1, pv[:, :], 5, 3)
            glu(1, 1, pm[:, 1, :], 7, 4)

            def gate_sum(i):
                r = raw_at["g", i]
                dve.wait_ge(s_raw[r % 3], raw_due[r])
                if i == 0:
                    dve.wait_ge(p_xT, 16)
                    ins = dve.tensor_scalar(gacc[:, :], raw[:, r % 3, :], cact[:, i:i + 1], None, ALU.mult)
                else:
                    dve.wait_ge(d_gp, i)
                    ins = dve.scalar_tensor_tensor(out=gacc[:, :], in0=raw[:, r % 3, :], scalar=cact[:, i:i + 1],
                                                   in1=gacc[:, :], op0=ALU.mult, op1=ALU.add)
                ins.then_inc(d_gp, 1)

            conv(2)
            for i in range(4):
                gate_sum(i)
                conv(1)
            glu(2, 0, pm[:, (10 - 6) % 3, :], 10, 5)
            conv(1)
            gate_sum(4)
            glu(2, 1, pm[:, (11 - 6) % 3, :], 11, 6)
            for i in range(5, 8):
                conv(1)
                gate_sum(i)
            conv(2)
            glu(3, 0, pm[:, (14 - 6) % 3, :], 14, 7)
            conv(2)
            glu(3, 1, pm[:, (15 - 6) % 3, :], 15, 8)
            dve.wait_ge(p_gcol, 1)
            dve.tensor_tensor(gcol[:, :], tr[:, 0, 0:KT], cols[:, C_GT:C_GT + KT], ALU.add).then_inc(d_gcol, 1)

            def bank(i):
                return pm[:, (i - 6) % 3, :]

            def sum_squares(t):
                dve.wait_ge(a_v, t + 1)
                if t:
                    dve.wait_ge(g_rs, t)
                dve.tensor_reduce(ssq[:, :], rot2[:, :].rearrange("p (h d) -> p h d", d=DH), AX.X, ALU.add).then_inc(d_ss, 1)

            def normalize_qk(t):
                dve.wait_ge(g_rs, t + 1)
                if t:
                    dve.wait_ge(g_rope, t)
                dve.tensor_tensor(qk[:, 0:512].rearrange("p (h d) -> p h d", d=DH),
                                  bank(16 + 2 * t).rearrange("p (h d) -> p h d", d=DH),
                                  rsq[:, 0:NH].unsqueeze(2).to_broadcast([P, NH, DH]), ALU.mult)
                dve.tensor_tensor(qk[:, 512:640].rearrange("p (h d) -> p h d", d=DH),
                                  bank(17 + 2 * t)[:, 0:P].rearrange("p (h d) -> p h d", d=DH),
                                  rsq[:, NH:NH + NKV].unsqueeze(2).to_broadcast([P, NKV, DH]), ALU.mult).then_inc(d_qn, 1)

            def previous_keys(b, jj):
                s = sel1 if b % 2 else sel0
                dve.wait_ge(a_sel, 2 * b + jj + 1)
                src = ps[:, :, :].rearrange("p g (j s n) -> p (g j) s n", j=2, s=2)[:, :, 1 - b % 2, :]
                dve.copy_predicated(s[:, 4 * jj:4 * jj + 4, :], later[:, :].unsqueeze(1).to_broadcast([P, 4, P]),
                                    src).then_inc(d_cp, 1)

            def row_max(b):
                s = sel1 if b % 2 else sel0
                if b == 0:
                    dve.wait_ge(g_blk0, 1)
                else:
                    dve.wait_ge(d_cp, 2 * b)
                if b >= 2:
                    dve.wait_ge(a_exp, b - 1)
                link(dve.tensor_reduce(nmx[:, b % 2, :], s[:, :, :], AX.X, ALU.max, negate=True))
                m = nmx[:, b % 2, :].rearrange("p (jj g jh) -> p jj g jh", jj=2, g=2)
                dve.tensor_tensor(m, m, nsnk_v, ALU.min).then_inc(d_nmx, 1)

            nsnk_v = nsnk[:, :].rearrange("p (g jj jh) -> p jj g jh", g=2, jj=2)

            def denominators(b):
                dve.wait_ge(g_den, b + 1)
                if b:
                    dve.wait_ge(a_pn, b)
                dve.reciprocal(rden[:, :], psum_p[:, :]).then_inc(d_rden, 1)

            def gate(m, half):
                i = 32 + 2 * m + half
                sl = slice(half * HALF, (half + 1) * HALF)
                dve.wait_ge(a_tanh, 8 + 2 * m + half + 1)
                dst = gb[:, m, sl] if m < NCT else obuf[:, half, :]
                dve.scalar_tensor_tensor(out=dst, in0=dst, scalar=1.0, in1=bank(i), op0=ALU.add,
                                         op1=ALU.mult).then_inc(d_gate, 1)
                if m >= NCT:
                    j = m - NCT
                    dve.wait_ge(d_gate, 2 * m + half + 1)
                    dve.wait_ge(a_att, NT)
                    dve.tensor_tensor(att[:, j, sl], att[:, j, sl], obuf[:, half, :], ALU.mult).then_inc(d_ya, 1)

            plan = [3, 3, 1, 1, 1, 1, 1, 1, 1, 1, 1, 1, 3, 3, 0, 0]
            rest = 2 * TAPS - done[0]
            for n in range(16):
                t, b2, b3 = n - 1, n - 2, n - 3
                if n > 8:
                    gate(n - 9, 0)
                    gate(n - 9, 1)
                if 0 <= t < NT:
                    conv(min(1, 2 * TAPS - done[0]))
                    sum_squares(t)
                    conv(min(1, 2 * TAPS - done[0]))
                    normalize_qk(t)
                if 0 <= b2 < NT:
                    conv(min(1, 2 * TAPS - done[0]))
                    if b2:
                        previous_keys(b2, 0)
                if 0 <= b3 < NT:
                    denominators(b3)
                if 0 <= b2 < NT:
                    conv(min(1, 2 * TAPS - done[0]))
                    if b2:
                        previous_keys(b2, 1)
                    row_max(b2)
                conv(min(plan[n], 2 * TAPS - done[0]))
                if n == 12:
                    dve.wait_ge(p_PT, 16)
                    dve.wait_ge(g_rope, NT)
                    dve.wait_ge(p_T, NT)
                    dve.tensor_tensor(gdiag[:, :, :], ident[:, :].unsqueeze(1).to_broadcast([P, KT, P]),
                                      gcol[:, :].unsqueeze(2).to_broadcast([P, KT, P]), ALU.mult).then_inc(d_gdiag, 1)
            conv(2 * TAPS - done[0])
            gate(7, 0)
            gate(7, 1)

            conv_out = [cacc[:, 0, :], cacc[:, 1, :], z[:, 0, 0:S], z[:, 1, 0:S]]
            dve.wait_ge(d_conv, 4 * TAPS)
            dve.tensor_tensor(lnbuf[:, 1, 0:S], conv_out[2], conv_out[3], ALU.add).then_inc(d_s23, 1)
            dve.wait_ge(p_mean, 1)
            for ct in range(NCT):
                dve.scalar_tensor_tensor(out=conv_out[ct], in0=ps[:, :, :].rearrange("p a n -> p (a n)"),
                                         scalar=-1.0 / 512, in1=conv_out[ct], op0=ALU.mult, op1=ALU.add).then_inc(d_dm, 1)
            dve.wait_ge(p_var, NCT)
            dve.tensor_copy(ssx[:, :], pv[:, 0:NT]).then_inc(d_var, 1)
            dve.wait_ge(g_rstd, 1)
            dve.tensor_tensor(lnbuf[:, 0, 0:S].rearrange("p (t n) -> p t n", t=NT),
                              ident[:, :].unsqueeze(1).to_broadcast([P, NT, P]),
                              rsx[:, :].unsqueeze(2).to_broadcast([P, NT, P]), ALU.mult).then_inc(d_ldiag, 1)
            dve.wait_ge(p_bc, 1)
            for ct in range(NCT):
                e = conv_out[ct]
                dve.wait_ge(a_sq, ct + 1)
                dve.tensor_tensor(e, e, ps[:, :, :].rearrange("p a n -> p (a n)"), ALU.mult).then_inc(d_e, 1)
                dve.wait_ge(a_ty, ct + 1)
                link(dve.tensor_scalar(e, e, lnc[:, 2, ct:ct + 1], lnc[:, 3, ct:ct + 1], ALU.mult, ALU.add))
                link(dve.scalar_tensor_tensor(out=lnbuf[:, 1, 0:S], in0=lnbuf[:, 1, 0:S], scalar=1.0, in1=e,
                                              op0=ALU.add, op1=ALU.mult))
                dve.tensor_tensor(gb[:, ct, :], gb[:, ct, :], lnbuf[:, 1, 0:S], ALU.mult).then_inc(d_yb, 1)

            obanks = [tr[:, 0, :], tr[:, 1, :], pm[:, 0, :], pm[:, 1, :], pm[:, 2, :]]
            for i in range(2 * NT):
                n = i // NT
                dve.wait_ge(p_out, i + 1)
                if i >= 2:
                    dve.wait_ge(g_fin, i - 1)
                dve.tensor_tensor(obuf[:, i % 2, :], obanks[i % 5], gbc[:, n * HALF:(n + 1) * HALF],
                                  ALU.mult).then_inc(d_o, 1)


def rope_table():
    inv = (10000.0 ** (-np.arange(0, DH, 2) / DH)).astype(np.float32)
    ang = np.arange(S, dtype=np.float32)[:, None] * inv[None, :]
    co, si = np.cos(ang), np.sin(ang)
    return np.ascontiguousarray(np.concatenate([co, co, -si, si], axis=1).astype(np.float32))


_INS = ["x", "c", "w_ada", "b_ada", "norm_w", "w_in", "q_norm_w", "k_norm_w", "sinks", "conv_w", "conv_b",
        "ln_w", "ln_b", "w_out"]


def kernel(**inputs):
    import concourse.bacc as bacc
    from concourse.bass_utils import run_bass_kernel_spmd

    nc = bacc.Bacc("TRN2", target_bir_lowering=False, num_devices=1)
    arrays = {f"in_{n}": np.ascontiguousarray(inputs[n]) for n in _INS}
    arrays["in_rope"] = rope_table()
    args = [nc.dram_tensor(n, a.shape, mybir.dt.from_np(a.dtype), kind="ExternalInput").ap() for n, a in arrays.items()]
    args.append(nc.dram_tensor("out_0", (1, S, D), F32, kind="ExternalOutput").ap())
    build(nc, *args)
    return run_bass_kernel_spmd(nc, [arrays], core_ids=[0]).results[0]["out_0"]
```

```python
from contextlib import ExitStack

import numpy as np

import concourse.bass as bass
from concourse import mybir

F32 = mybir.dt.float32
F32R = mybir.dt.float32r
U8 = mybir.dt.uint8
ALU = mybir.AluOpType
ACT = mybir.ActivationFunctionType
AX = mybir.AxisListType

P = 128
D = 1024
S = 1024
HALF = 512
KT = D // P
NT = S // P
DH = 64
NH = 8
NKV = 2
GRP = NH // NKV
TAPS = 31
PAD = TAPS - 1
ZW = S + 32
NCT = 4
EPS = 1e-6
FILL = -1.0e38
U = 256
Q0, K0, GA0, A0, G0, GB0 = 0, 512, 768, 1280, 1792, 2304


def build(nc, x, c, w_ada, b_ada, norm_w, w_in, q_norm_w, k_norm_w, sinks,
          conv_w, conv_b, ln_w, ln_b, w_out, rope_rows, out):
    base = 16512

    def at(name, shape, dtype, offset):
        return nc.alloc_sbuf_tensor_at(name, [P] + shape, dtype, offset=base + offset)

    H_AT, W_AT, RAW_AT, XG_AT, C_AT, S_AT = 0, 65536, 131072, 143360, 176128, 201216
    Z_AT = W_AT
    h = at("h", [2, KT, S], F32R, H_AT)
    wts = at("wts", [4, 2, KT, U], F32R, W_AT)
    sel0 = at("sel0", [NH, P], F32, Z_AT)
    pcur = [at("pcur0", [GRP, P], F32, Z_AT + 4096), at("pcur1", [GRP, P], F32, XG_AT + 24576)]
    pprev = [at("pprev0", [GRP, P], F32, Z_AT + 6144), at("pprev1", [GRP, P], F32, XG_AT + 26624)]
    qk = at("qk", [10 * DH], F32, Z_AT + 8192)
    rot1 = at("rot1", [10 * DH], F32, Z_AT + 10752)
    rot2 = at("rot2", [10 * DH], F32, Z_AT + 13312)
    lnA = at("lnA", [S], F32, Z_AT)
    lnB = at("lnB", [S], F32, Z_AT + 4096)
    vrows = at("vrows", [P], F32, Z_AT)
    cwrows = at("cwrows", [512], F32, Z_AT + 512)
    h32 = at("h32", [2, HALF], F32, Z_AT + 2560)
    junk = at("junk", [D], F32, Z_AT + 6656)
    ada_acc = at("ada_acc", [2, 2, 2 * P], F32, Z_AT + 10752)
    gdiag = at("gdiag", [NT, P], F32, Z_AT + 8192)
    raw = at("raw", [3, 1024], F32, RAW_AT)
    xs = at("xs", [NT, D], F32, XG_AT)
    att = at("att", [NCT, S], F32, XG_AT)
    gb = at("gb", [NCT, S], F32, XG_AT + 16384)
    gacc = at("gacc", [D], F32, XG_AT + 16384)
    sel1 = at("sel1", [NH, P], F32, XG_AT + 16384 + 12288)
    xr = at("xr", [NT, D], F32, XG_AT)
    z = at("z", [NCT, ZW], F32, C_AT)
    cacc = at("cacc", [2, S], F32, C_AT + 4 * 4 * ZW)
    slab = at("slab", [3, KT, 2, P], F32, C_AT)
    lnbuf = at("lnbuf", [2, ZW], F32, C_AT + 2 * 4 * ZW)
    v = at("v", [5, P], F32, S_AT)
    qT = at("qT", [GRP, P], F32, S_AT + 2560)
    kT = at("kT", [2, P], F32, S_AT + 4608)
    ropr = at("ropr", [P], F32, S_AT + 5632)
    tab = at("tab", [2, 2, NKV, DH], F32, S_AT + 6144)
    gbc = at("gbc", [D], F32, S_AT)
    obuf = at("obuf", [2, HALF], F32, S_AT + 4096)
    spot = [S_AT + 8192]

    def small(name, shape, dtype=F32):
        t = at(name, shape, dtype, spot[0])
        n = int(np.prod(shape)) * (1 if dtype == U8 else 4)
        spot[0] += -(-n // 32) * 32
        return t

    ident = small("ident", [P])
    ones = small("ones", [P])
    later = small("later", [P], U8)
    cols = small("cols", [52])
    cw = small("cw", [NCT, TAPS])
    wqk = small("wqk", [NKV, DH])
    snk = small("snk", [NH])
    nsnk = small("nsnk", [NH])
    mhalf = small("mhalf", [10])
    cact = small("cact", [KT])
    tiny = small("tiny", [12])
    ssx = small("ssx", [NT])
    rsx = small("rsx", [NT])
    ssq = small("ssq", [10])
    rsq = small("rsq", [10])
    modA = small("modA", [KT])
    modB = small("modB", [KT])
    bs1 = small("bs1", [KT])
    gcol = small("gcol", [KT])
    nmx = small("nmx", [2, NH])
    sdiff = small("sdiff", [NH])
    esink = small("esink", [NH])
    psum_p = small("psum_p", [NH])
    rden = small("rden", [NH])
    lnc = small("lnc", [4, NCT])
    assert spot[0] <= 229344 - base, spot[0]
    C_C, C_NW, C_SH, C_SC, C_GT, C_CB, C_LW, C_LB = 0, 8, 16, 24, 32, 40, 44, 48

    with ExitStack() as ctx:
        def psum(name, shape):
            return ctx.enter_context(nc.psum_tensor(name, [P] + shape, F32))

        def sem(name):
            return ctx.enter_context(nc.semaphore(name))

        pm = psum("pm", [3, HALF])
        ps = psum("ps", [2, HALF])
        tr = psum("tr", [2, HALF])
        pv = psum("pv", [HALF])

        s_vec, s_cw, s_bc = sem("s_vec"), sem("s_cw"), sem("s_bc")
        s_x = [sem(f"s_x{t}") for t in range(NT)]
        s_slab = [sem(f"s_slab{i}") for i in range(3)]
        s_raw = [sem(f"s_raw{i}") for i in range(3)]
        s_rope = sem("s_rope")
        s_xr = [sem(f"s_xr{t}") for t in range(NT)]
        s_out = sem("s_out")
        g_const, g_rsx, g_lo, g_tab = sem("g_const"), sem("g_rsx"), sem("g_lo"), sem("g_tab")
        g_rs, g_mask, g_rope = sem("g_rs"), sem("g_mask"), sem("g_rope")
        g_blk0, g_ylo, g_fin, g_link = sem("g_blk0"), sem("g_ylo"), sem("g_fin"), sem("g_link")
        g_s01, g_rstd = sem("g_s01"), sem("g_rstd")
        p_rows, p_xT, p_ada, p_main = sem("p_rows"), sem("p_xT"), sem("p_ada"), sem("p_main")
        p_gcol, p_gbc, p_T, p_S, p_PT, p_PV = sem("p_gcol"), sem("p_gbc"), sem("p_T"), sem("p_S"), sem("p_PT"), sem("p_PV")
        p_mean, p_sq, p_var, p_bc, p_out = sem("p_mean"), sem("p_sq"), sem("p_var"), sem("p_bc"), sem("p_out")
        a_lv = sem("a_lv")
        a_cols, a_ssx, a_h32, a_hi, a_tanh = sem("a_cols"), sem("a_ssx"), sem("a_h32"), sem("a_hi"), sem("a_tanh")
        a_v, a_pt, a_exp, a_qT, a_sel = sem("a_v"), sem("a_pt"), sem("a_exp"), sem("a_qT"), sem("a_sel")
        a_pn, a_att, a_yhi, a_gbc, a_sq, a_ty = sem("a_pn"), sem("a_att"), sem("a_yhi"), sem("a_gbc"), sem("a_sq"), sem("a_ty")
        a_link = sem("a_link")
        d_cact, d_xn, d_ada, d_ab, d_hhi, d_hlo = sem("d_cact"), sem("d_xn"), sem("d_ada"), sem("d_ab"), sem("d_hhi"), sem("d_hlo")
        d_glu, d_conv, d_gp, d_gcol, d_ss, d_qn = sem("d_glu"), sem("d_conv"), sem("d_gp"), sem("d_gcol"), sem("d_ss"), sem("d_qn")
        d_cp, d_nmx, d_rden, d_gate, d_ya = sem("d_cp"), sem("d_nmx"), sem("d_rden"), sem("d_gate"), sem("d_ya")
        d_gdiag, d_s23, d_dm, d_var, d_ldiag, d_e, d_v, d_yb, d_o, d_link = (
            sem("d_gdiag"), sem("d_s23"), sem("d_dm"), sem("d_var"), sem("d_ldiag"), sem("d_e"), sem("d_v"),
            sem("d_yb"), sem("d_o"), sem("d_link"))

        units = [(w_in, A0), (w_in, G0), (w_in, G0 + U), (w_in, A0 + U), (w_in, Q0), (w_in, Q0 + U), (w_in, K0),
                 (w_in, GB0), (w_in, GB0 + U), (w_in, GA0), (w_in, GA0 + U),
                 (w_out, U), (w_out, 0), (w_out, 2 * U), (w_out, 3 * U)]
        slots = [1, 2, 3, 1, 2, 3, 1, 2, 3, 1, 2, 3, 1, 0, 2]
        used = [8, 8, 14, 16, 31, 31, 32, 36, 40, 44, 48]
        free = [0, 0, 0, used[0], used[1], used[2], used[3], used[4], used[5], used[6], used[7],
                used[8], used[9], 0, used[10]]
        pieces = [(0, 0), (1, 0), (0, 1), (1, 1)] + [(u, p) for u in range(2, len(units)) for p in range(2)]
        raws = [("w", i) for i in range(10)] + [("g", i) for i in range(KT)] + [("w", i) for i in range(10, len(pieces))]
        raw_at = {key: r for r, key in enumerate(raws)}

        def transfers(u, p):
            src, c0 = units[u]
            if src is w_in:
                return 4 if GA0 <= c0 < A0 else 1
            return 2 if p == 0 else 1

        raw_due = []
        total = [0, 0, 0]
        for r, (kind, i) in enumerate(raws):
            total[r % 3] += 16 * (transfers(*pieces[i]) if kind == "w" else 1)
            raw_due.append(total[r % 3])

        def split_done(u, p=1):
            return pieces.index((u, p)) + 1

        def whalf(i):
            u, p = pieces[i]
            return slots[u], slice(4 * p, 4 * p + 4)

        y_order = [(k, half) for k0 in (0, NCT) for half in range(2) for k in range(k0, k0 + NCT)]

        def y_src(k, sl):
            return att[:, k, sl] if k < NCT else gb[:, k - NCT, sl]

        conv_out = [cacc[:, 0, :], cacc[:, 1, :], z[:, 0, 0:S], z[:, 1, 0:S]]
        sq = [lnbuf[:, 0, 0:S], lnbuf[:, 1, 0:S], lnA[:, :], lnB[:, :]]

        block = ctx.enter_context(nc.Block())

        @block.sync
        def _(sp):
            k0 = 0
            for vec, n in ((c, 8), (norm_w, 8), (b_ada, 24), (conv_b, 4), (ln_w, 4), (ln_b, 4)):
                sp.dma_start(vrows[k0:k0 + n, :], vec[0].rearrange("(r p) -> r p", p=P)).then_inc(s_vec, 16)
                k0 += n
            for t in range(4):
                sp.dma_start(xs[:, t, :], x[0, t * P:(t + 1) * P, :]).then_inc(s_x[t], 16)

            def load_raw(r):
                kind, i = raws[r]
                if r >= 3:
                    was, n = raws[r - 3]
                    sp.wait_ge(g_lo if was == "w" else d_gp, n + 1)
                dst = raw[:, r % 3, :]
                if kind == "g":
                    sp.dma_start(dst, w_ada[0, i * P:(i + 1) * P, 2 * D:3 * D]).then_inc(s_raw[r % 3], 16)
                    return
                u, p = pieces[i]
                src, c0 = units[u]
                if src is w_out and p == 0:
                    for g in range(NKV):
                        sp.dma_start(raw[g * DH:(g + 1) * DH, r % 3, :].rearrange("p (k n) -> p k n", k=4),
                                     src[0, g * 256:(g + 1) * 256, c0:c0 + U].rearrange("(k p) n -> p k n", p=DH)
                                     ).then_inc(s_raw[r % 3], 16)
                    return
                if transfers(u, p) == 4:
                    for j in range(2):
                        for g in range(NKV):
                            first = GA0 + (4 * g + 2 * ((c0 - GA0) // U) + j) * DH
                            sp.dma_start(dst.rearrange("p (k j g d) -> p k j g d", k=4, j=2, g=NKV)[:, :, j, g, :],
                                         src[0, p * 512:(p + 1) * 512, first:first + DH].rearrange("(k p) d -> p k d", p=P)
                                         ).then_inc(s_raw[r % 3], 16)
                    return
                sp.dma_start(dst.rearrange("p (k n) -> p k n", k=4),
                             src[0, p * 512:(p + 1) * 512, c0:c0 + U].rearrange("(k p) n -> p k n", p=P)
                             ).then_inc(s_raw[r % 3], 16)

            def load_slab(k):
                if k >= 3:
                    sp.wait_ge(p_ada, k - 2)
                for part in range(2):
                    sp.dma_start(slab[:, k % 3, :, part, :],
                                 w_ada[0, :, part * D + k * P:part * D + (k + 1) * P].rearrange("(t p) n -> p t n", p=P)
                                 ).then_inc(s_slab[k % 3], 16)

            load_raw(0)
            load_raw(1)
            load_slab(0)
            sp.dma_start(cwrows[0:TAPS, :], conv_w[0]).then_inc(s_cw, 16)
            load_slab(1)
            load_raw(2)
            load_slab(2)
            load_raw(3)
            sp.dma_start(wqk[:, 0, :], q_norm_w.to_broadcast([P, DH])).then_inc(s_bc, 16)
            sp.dma_start(wqk[:, 1, :], k_norm_w.to_broadcast([P, DH])).then_inc(s_bc, 16)
            sp.dma_start(snk[:, :], sinks.to_broadcast([P, NH])).then_inc(s_bc, 16)
            for k in range(3, KT):
                load_slab(k)
            for t in range(4, NT):
                sp.dma_start(xs[:, t, :], x[0, t * P:(t + 1) * P, :]).then_inc(s_x[t], 16)

            def load_rope(t):
                if t:
                    sp.wait_ge(g_tab, t)
                sp.dma_start(ropr[:, :], rope_rows[t * P:(t + 1) * P, :]).then_inc(s_rope, 16)

            r = 4
            while raws[r] != ("w", 12):
                load_raw(r)
                r += 1
            load_rope(0)
            load_raw(r)
            load_raw(r + 1)
            r += 2
            for t in range(1, NT):
                load_rope(t)
            while r < len(raws):
                load_raw(r)
                r += 1
                if raws[r - 1] == ("w", 28):
                    for t in range(NT):
                        sp.wait_ge(g_ylo, 4 + t % 4 + 1 + (8 if t >= 4 else 0))
                        sp.dma_start(xr[:, t, :], x[0, t * P:(t + 1) * P, :]).then_inc(s_xr[t], 16)
            for i in range(2 * NT):
                sp.wait_ge(g_fin, i + 1)
                t, n = i % NT, i // NT
                sp.dma_start(out[0, t * P:(t + 1) * P, n * HALF:(n + 1) * HALF],
                             xr[:, t, n * HALF:(n + 1) * HALF]).then_inc(s_out, 16)
            sp.wait_ge(s_out, 16 * 2 * NT)

        @block.gpsimd
        def _(gp):
            linked = [0]

            def link(ins):
                linked[0] += 1
                ins.then_inc(g_link, 1)
                gp.wait_ge(g_link, linked[0])

            gp.memset(ones[:, :], 1.0).then_inc(g_const, 1)
            gp.memset(mhalf[:, :], -0.5).then_inc(g_const, 1)
            gp.wait_ge(g_const, 2)
            gp.affine_select(out=ident[:, :], in_=ones[:, :], compare_op=ALU.is_equal, fill=0.0,
                             base=0, pattern=[[-1, P]], channel_multiplier=1).then_inc(g_const, 1)
            link(gp.affine_select(out=junk[:, 0:P], in_=ones[:, :], compare_op=ALU.is_gt, fill=0.0,
                                  base=0, pattern=[[1, P]], channel_multiplier=-1))
            gp.tensor_copy(later[:, :], junk[:, 0:P]).then_inc(g_const, 1)

            def rms_x(half):
                gp.wait_ge(a_ssx, 4 * half + 4)
                sl = slice(4 * half, 4 * half + 4)
                link(gp.tensor_scalar(tiny[:, 0:4], ssx[:, sl], 1.0 / D, EPS, ALU.mult, ALU.add))
                gp.tensor_tensor(rsx[:, sl], tiny[:, 0:4], mhalf[:, 0:4], ALU.pow).then_inc(g_rsx, 1)

            def w_lo(i):
                gp.wait_ge(a_hi, i + 1)
                slot, ks = whalf(i)
                gp.tensor_tensor(wts[:, slot, 1, ks, :],
                                 raw[:, raw_at["w", i] % 3, :].rearrange("p (k n) -> p k n", k=4),
                                 wts[:, slot, 0, ks, :].bitcast(F32), ALU.subtract).then_inc(g_lo, 1)

            rms_x(0)
            for i in range(4):
                w_lo(i)
            gp.wait_ge(s_bc, 48)
            link(gp.tensor_scalar(wqk[:, 0, :], wqk[:, 0, :], DH ** -0.5, None, ALU.mult))
            link(gp.tensor_scalar(nsnk[:, :], snk[:, :], -1.0, None, ALU.mult))
            rms_x(1)
            for i in range(4, 10):
                w_lo(i)

            def tables(t):
                gp.wait_ge(s_rope, 16 * (t + 1))
                if t >= 2:
                    gp.wait_ge(g_rope, t - 1)
                cc = ropr[:, 0:DH].unsqueeze(1).to_broadcast([P, NKV, DH])
                gp.tensor_tensor(tab[:, t % 2, 0, :, :], cc, wqk[:, :, :], ALU.mult)
                for lo, other in ((0, 32), (32, 0)):
                    ss = ropr[:, DH + lo:DH + lo + 32].unsqueeze(1).to_broadcast([P, NKV, 32])
                    last = gp.tensor_tensor(tab[:, t % 2, 1, :, lo:lo + 32], ss, wqk[:, :, other:other + 32], ALU.mult)
                last.then_inc(g_tab, 1)

            def rms_qk(t):
                gp.wait_ge(d_ss, t + 1)
                if t:
                    gp.wait_ge(d_qn, t)
                link(gp.tensor_scalar(tiny[:, 0:10], ssq[:, :], 1.0 / DH, EPS, ALU.mult, ALU.add))
                gp.tensor_tensor(rsq[:, :], tiny[:, 0:10], mhalf[:, :], ALU.pow).then_inc(g_rs, 1)

            def rope(t):
                gp.wait_ge(d_qn, t + 1)
                gp.wait_ge(g_tab, t + 1)
                if t:
                    gp.wait_ge(p_T, t)
                q, k = slice(0, 512), slice(512, 640)
                for i, part, grp, n in ((0, q, NKV, GRP), (1, k, 1, NKV)):
                    src = qk[:, part].rearrange("p (g j d) -> p g j d", g=grp, d=DH)
                    r1 = rot1[:, part].rearrange("p (j g d) -> p g j d", g=grp, d=DH)
                    r2 = rot2[:, part].rearrange("p (j g d) -> p g j d", g=grp, d=DH)
                    co = tab[:, t % 2, 0, i, :].unsqueeze(1).unsqueeze(1).to_broadcast([P, grp, n, DH])
                    gp.tensor_tensor(r1, src, co, ALU.mult)
                    for lo, other in ((0, 32), (32, 0)):
                        si = tab[:, t % 2, 1, i, lo:lo + 32].unsqueeze(1).unsqueeze(1).to_broadcast([P, grp, n, 32])
                        last = gp.tensor_tensor(r2[:, :, :, lo:lo + 32], src[:, :, :, other:other + 32], si, ALU.mult)
                link(last)
                gp.tensor_tensor(rot1[:, :], rot1[:, :], rot2[:, :], ALU.add).then_inc(g_rope, 1)

            def masks(b, g):
                gp.wait_ge(a_pt, 2 * b + g + 1)
                if b:
                    gp.affine_select(out=pprev[g][:, :, :], in_=pcur[g][:, :, :], compare_op=ALU.is_gt, fill=0.0,
                                     base=0, pattern=[[0, GRP], [-1, P]], channel_multiplier=1).then_inc(g_link, 1)
                    linked[0] += 1
                    gp.wait_ge(g_link, linked[0])
                gp.affine_select(out=pcur[g][:, :, :], in_=pcur[g][:, :, :], compare_op=ALU.is_ge, fill=0.0,
                                 base=0, pattern=[[0, GRP], [1, P]], channel_multiplier=-1).then_inc(g_mask, 1)

            tables(0)
            for i in range(10, 14):
                w_lo(i)
            for n in range(12):
                b2, b4, t = n - 2, n - 4, n - 1
                if 0 <= b4 < NT:
                    masks(b4, 0)
                    masks(b4, 1)
                if 0 <= t < NT:
                    rms_qk(t)
                    rope(t)
                if b2 == 0:
                    gp.wait_ge(a_sel, 2)
                    gp.affine_select(out=sel0[:, :, :], in_=sel0[:, :, :], compare_op=ALU.is_ge, fill=FILL,
                                     base=0, pattern=[[0, NH], [-1, P]], channel_multiplier=1).then_inc(g_blk0, 1)
                if n + 1 < NT:
                    tables(n + 1)
                if 7 <= n < 11:
                    w_lo(2 * n)
                    w_lo(2 * n + 1)
            gp.wait_ge(d_conv, 2 * TAPS)
            gp.wait_ge(p_PV, 16)
            gp.tensor_tensor(lnA[:, :], cacc[:, 0, :], cacc[:, 1, :], ALU.add).then_inc(g_s01, 1)
            for i in range(22, 26):
                w_lo(i)
            gp.wait_ge(d_var, 1)
            link(gp.tensor_scalar(tiny[:, 0:8], ssx[:, :], 1.0 / (512 * 32), EPS, ALU.mult, ALU.add))
            gp.tensor_tensor(rsx[:, :], tiny[:, 0:8], mhalf[:, 0:8], ALU.pow).then_inc(g_rstd, 1)
            for i, (k, half) in enumerate(y_order):
                gp.wait_ge(a_yhi, i + 1)
                sl = slice(half * HALF, (half + 1) * HALF)
                gp.tensor_tensor(h[:, 1, k, sl], y_src(k, sl), h[:, 0, k, sl].bitcast(F32),
                                 ALU.subtract).then_inc(g_ylo, 1)
            for i in range(26, 30):
                w_lo(i)

            for i in range(2 * NT):
                gp.wait_ge(d_o, i + 1)
                t, n = i % NT, i // NT
                gp.wait_ge(s_xr[t], 16)
                sl = slice(n * HALF, (n + 1) * HALF)
                gp.tensor_tensor(xr[:, t, sl], xr[:, t, sl], obuf[:, i % 2, :], ALU.add).then_inc(g_fin, 1)

        @block.tensor
        def _(pe):
            pe.wait_ge(g_const, 4)
            pe.wait_ge(s_vec, 96)
            pe.transpose(pv[:, 0:52], vrows[0:52, :], ident[0:52, 0:52]).then_inc(p_rows, 1)

            def x_transposes(idx):
                half, k = idx // KT, idx % KT
                if k == 0:
                    pe.wait_ge(d_xn, 4 * half + 4)
                if idx >= 2:
                    pe.wait_ge(a_h32, idx - 1)
                for t in range(4):
                    last = pe.transpose(tr[:, k % 2, t * P:(t + 1) * P], xs[:, 4 * half + t, k * P:(k + 1) * P], ident[:, :])
                last.then_inc(p_xT, 1)

            def ada_bank(k):
                return pv if k % 2 == 0 else ps[:, 1, :]

            def ada_cols(k):
                if k == 0:
                    pe.wait_ge(d_cact, 1)
                    pe.wait_ge(a_cols, 3)
                if k >= 2:
                    pe.wait_ge(d_ab, 2 * (k - 1))
                pe.wait_ge(s_slab[k % 3], 32 * (k // 3 + 1))
                pe.wait_ge(d_ada, 6 * k + 6)
                for part in range(2):
                    o = ada_bank(k)[:, part:part + 1]
                    for ct in (6, 7):
                        pe.matmul(o, slab[:, k % 3, ct, part, :], cact[:, ct:ct + 1], start=(ct == 6), stop=False)
                    for ch in range(2):
                        last = pe.matmul(o, ada_acc[:, k % 2, ch, part * P:(part + 1) * P], ones[:, 0:1],
                                         start=False, stop=(ch == 1))
                last.then_inc(p_ada, 1)

            def three(out, hi_w, lo_w, hi_x, lo_x, first, last):
                pe.matmul(out, hi_w, hi_x, start=first, stop=False)
                pe.matmul(out, lo_w, hi_x, start=False, stop=False)
                return pe.matmul(out, hi_w, lo_x, start=False, stop=last)

            def channel_step(out, slot, col, half, k):
                sl = slice(half * HALF, (half + 1) * HALF)
                return three(out, wts[:, slot + 1, 0, k, col:col + P], wts[:, slot + 1, 1, k, col:col + P],
                             h[:, 0, k, sl], h[:, 1, k, sl], k == 0, k == KT - 1)

            x_transposes(0)
            pe.wait_ge(s_cw, 16)
            pe.wait_ge(a_cols, 1)
            for i in range(NCT):
                last = pe.transpose(pv[:, 64 + 32 * i:64 + 32 * i + TAPS], cwrows[0:TAPS, i * P:(i + 1) * P],
                                    ident[0:TAPS, 0:TAPS])
            last.then_inc(p_rows, 1)
            ada_cols(0)
            early = [(pm[:, 0, :], 1, 0), (pm[:, 1, :], 1, P), (pm[:, 2, :], 0, 0), (ps[:, 0, :], 0, P)]
            for k in range(KT):
                if k + 1 < KT:
                    x_transposes(k + 1)
                    ada_cols(k + 1)
                pe.wait_ge(d_hlo, k + 1)
                if k % 4 == 0:
                    pe.wait_ge(g_lo, 2 if k == 0 else 4)
                for bank, slot, col in early:
                    last = channel_step(bank, slot, col, 0, k)
                    if k == KT - 1:
                        last.then_inc(p_main, 1)
            for k in range(KT):
                x_transposes(KT + k)

            def channel_tile(out, slot, col, half):
                for k in range(KT):
                    if half == 1:
                        pe.wait_ge(d_hlo, KT + k + 1)
                    last = channel_step(out, slot, col, half, k)
                return last

            pe.wait_ge(d_ab, 16)
            channel_tile(ps[:, 1, :], 1, 0, 1).then_inc(p_main, 1)
            channel_tile(pv[:, :], 0, 0, 1).then_inc(p_main, 1)
            pe.wait_ge(a_tanh, 1)
            channel_tile(pm[:, 0, :], 1, P, 1).then_inc(p_main, 1)
            pe.wait_ge(a_tanh, 2)
            channel_tile(pm[:, 1, :], 0, P, 1).then_inc(p_main, 1)

            def bank(i):
                return pm[:, (i - 6) % 3, :]

            def wait_bank(i):
                j = i - 3
                if j == 5:
                    pe.wait_ge(d_glu, 1)
                elif j == 6:
                    pe.wait_ge(a_tanh, 4)
                elif j == 7:
                    pe.wait_ge(d_glu, 4)
                elif j < 16:
                    pair, part = (j - 8) // 4, (j - 8) % 4
                    if part < 2:
                        pe.wait_ge(a_tanh, 4 + 2 * pair + part + 1)
                    else:
                        pe.wait_ge(d_glu, 4 + 2 * pair + part - 1)
                elif j < 32:
                    pe.wait_ge(a_v, (j - 16) // 2 + 1)
                else:
                    pe.wait_ge(d_gate, j - 31)

            use = 8
            for pair in range(2):
                for slot in (2, 0):
                    if pair == 0:
                        pe.wait_ge(g_lo, split_done(2 if slot == 2 else 3))
                    for half in range(2):
                        wait_bank(use)
                        for k in range(KT):
                            last = channel_step(bank(use), slot, pair * P, half, k)
                        last.then_inc(p_main, 1)
                        use += 1
            pe.wait_ge(d_gp, KT)
            pe.wait_ge(a_h32, 16)
            for i in range(KT):
                last = pe.matmul(tr[:, 0, i:i + 1], gacc[:, i * P:(i + 1) * P], ones[:, 0:1], start=True, stop=True)
            last.then_inc(p_gcol, 1)

            def transpose_qk(b):
                pe.wait_ge(g_rope, b + 1)
                if b == 0:
                    pe.wait_ge(d_gcol, 1)
                else:
                    pe.wait_ge(a_qT, b)
                if b >= 2:
                    pe.wait_ge(a_pt, 2 * (b - 1))
                for j in range(GRP):
                    pe.transpose(tr[:, 0, j * P:(j + 1) * P], rot1[:, j * P:(j + 1) * P], ident[:, :])
                pe.transpose(tr[:, 1, 0:P], rot1[:, 512:640], ident[:, :]).then_inc(p_T, 1)

            def scores(b, jj):
                pe.wait_ge(a_qT, b + 1)
                if b == 0 and jj == 0:
                    pe.wait_ge(d_glu, 2)
                    pe.wait_ge(a_tanh, 3)
                if 2 * b + jj:
                    pe.wait_ge(a_sel, 2 * b + jj)
                if 2 * (b - 1) + jj > 0:
                    pe.wait_ge(d_cp, 2 * (b - 1) + jj)
                for jh in range(2):
                    for g in range(NKV):
                        lhs = qT[g * DH:(g + 1) * DH, 2 * jj + jh, :]
                        if b:
                            o, rhs = ps[:, g, jh * 256:(jh + 1) * 256], kT[g * DH:(g + 1) * DH, :, :]
                        else:
                            o, rhs = ps[:, g, jh * 256:jh * 256 + P], kT[g * DH:(g + 1) * DH, 0, :]
                        last = pe.matmul(o, lhs, rhs, start=True, stop=True)
                last.then_inc(p_S, 1)

            def transpose_p(b):
                pe.wait_ge(a_pn, b + 1)
                pe.wait_ge(a_qT, min(b + 2, NT))
                if b:
                    pe.wait_ge(a_pt, 2 * b)
                s = sel1 if b % 2 else sel0
                for g in range(NKV):
                    for j in range(GRP):
                        last = pe.transpose(tr[:, g, j * P:(j + 1) * P], s[:, (j // 2) * 4 + g * 2 + j % 2, :], ident[:, :])
                    last.then_inc(p_PT, 1)

            def times_v(b, g):
                pe.wait_ge(g_mask, 2 * b + g + 1)
                pe.wait_ge(a_v, b + 1)
                if b:
                    pe.wait_ge(a_att, b)
                else:
                    pe.wait_ge(d_glu, 3)
                o = pv[g * DH:(g + 1) * DH, :]
                last = pe.matmul(o, v[:, b % 5, g * DH:(g + 1) * DH], pcur[g][:, :, :], start=True, stop=(b == 0))
                if b:
                    last = pe.matmul(o, v[:, (b - 1) % 5, g * DH:(g + 1) * DH], pprev[g][:, :, :], start=False, stop=True)
                last.then_inc(p_PV, 1)

            def attention_step(n, s):
                new, old = n - 2, n - 4
                if 0 <= old < NT:
                    if s == 0:
                        transpose_p(old)
                    if s == 4:
                        times_v(old, 0)
                    if s == 6:
                        times_v(old, 1)
                if 0 <= new < NT:
                    if s == 5:
                        transpose_qk(new)
                    if s == 8:
                        scores(new, 0)
                    if s == 12:
                        scores(new, 1)

            pe.wait_ge(g_lo, split_done(5))
            for t in range(NT):
                ts = slice(t * P, (t + 1) * P)
                for part in range(2):
                    i = 16 + 2 * t + part
                    for k in range(KT):
                        if t == 0 and part == 1 and k % 4 == 0:
                            pe.wait_ge(g_lo, split_done(6, k // 4))
                        attention_step(t, part * KT + k)
                        if k == 0:
                            wait_bank(i)
                        if part == 0:
                            o = bank(i).rearrange("p (s n) -> p s n", s=2)
                            w_hi, w_lo = wts[:, 2:4, 0, k, :], wts[:, 2:4, 1, k, :]
                        else:
                            o = bank(i)[:, 0:256]
                            w_hi, w_lo = wts[:, 1, 0, k, :], wts[:, 1, 1, k, :]
                        x_hi, x_lo = h[:, 0, k, ts], h[:, 1, k, ts]
                        pe.matmul(o, x_hi, w_hi, start=(k == 0), stop=False)
                        pe.matmul(o, x_hi, w_lo, start=False, stop=False)
                        last = pe.matmul(o, x_lo, w_hi, start=False, stop=(k == KT - 1))
                    last.then_inc(p_main, 1)

            def gate_row():
                pe.wait_ge(d_gdiag, 1)
                pe.wait_ge(a_pt, 2 * NT)
                for half in range(2):
                    last = pe.matmul(tr[:, half, :], ones[:, :], gdiag[:, 4 * half:4 * half + 4, :], start=True, stop=True)
                last.then_inc(p_gbc, 1)

            def ln_mean():
                pe.wait_ge(g_s01, 1)
                pe.wait_ge(d_s23, 1)
                pe.wait_ge(d_cp, 14)
                for half in range(2):
                    sl = slice(half * HALF, (half + 1) * HALF)
                    pe.matmul(ps[:, half, :], ones[:, :], lnA[:, sl], start=True, stop=False)
                    last = pe.matmul(ps[:, half, :], ones[:, :], lnB[:, sl], start=False, stop=True)
                last.then_inc(p_mean, 1)

            def ln_squares():
                pe.wait_ge(a_sq, NCT)
                pe.wait_ge(d_dm, NCT)
                for half in range(2):
                    sl = slice(half * HALF, (half + 1) * HALF)
                    for ct in range(NCT):
                        last = pe.matmul(ps[32 * ct:32 * ct + 32, half, :], ones[:, 0:32], sq[ct][:, sl],
                                         start=True, stop=True)
                last.then_inc(p_sq, 1)

            def ln_var():
                pe.wait_ge(a_lv, 1)
                pe.wait_ge(a_att, NT)
                for t in range(NT):
                    last = pe.matmul(pv[:, t:t + 1], lnA[:, t * P:(t + 1) * P], ones[:, 0:1], start=True, stop=True)
                last.then_inc(p_var, 1)

            for m in range(2 * NCT):
                n = NT + m
                for half in range(2):
                    i = 32 + 2 * m + half
                    for k in range(KT):
                        attention_step(n, half * KT + k)
                        if (m, half, k) == (5, 0, 0):
                            gate_row()
                        if (m, half, k) == (6, 0, 0):
                            ln_mean()
                        if (m, half, k) == (7, 0, 0):
                            ln_squares()
                        if (m, half, k) == (7, 1, 0):
                            ln_var()
                        if k == 0:
                            wait_bank(i)
                        if half == 0 and m % 2 == 0 and k % 4 == 0:
                            pe.wait_ge(g_lo, split_done(7 + m // 2, k // 4))
                        last = channel_step(bank(i), (1 + m // 2) % 3, (m % 2) * P, half, k)
                    last.then_inc(p_main, 1)

            obanks = [tr[:, 0, :], tr[:, 1, :], pm[:, 0, :], pm[:, 1, :], pm[:, 2, :]]

            def out_step(i, k):
                t, n = i % NT, i // NT
                ts = slice(t * P, (t + 1) * P)
                o = obanks[i % 5].rearrange("p (s n) -> p s n", s=2)
                w = [wts[:, (1 - n):4:2, part, k, :] for part in range(2)]
                pe.matmul(o, h[:, 0, k, ts], w[0], start=(k == 0), stop=False)
                pe.matmul(o, h[:, 0, k, ts], w[1], start=False, stop=False)
                return pe.matmul(o, h[:, 1, k, ts], w[0], start=False, stop=(k == KT - 1))

            def wait_y(k, half):
                pe.wait_ge(g_ylo, y_order.index((k, half)) + 1)

            pe.wait_ge(g_lo, split_done(12))
            pe.wait_ge(a_gbc, 1)
            for i in range(5):
                if i >= 2:
                    pe.wait_ge(d_gate, 14 + i - 2)
                for k in range(NCT):
                    if i % 4 == 0:
                        wait_y(k, i // 4)
                    out_step(i, k)
                if i == 1:
                    pe.wait_ge(d_ldiag, 1)
                    for half in range(2):
                        last = pe.matmul(ps[:, half, :], ones[:, :], lnbuf[:, 0, half * HALF:(half + 1) * HALF],
                                         start=True, stop=True)
                    last.then_inc(p_bc, 1)
            for i in range(2 * NT):
                if i >= 5:
                    pe.wait_ge(d_o, i - 4)
                if i == NT:
                    pe.wait_ge(g_lo, split_done(14))
                for k in range(NCT if i < 5 else 0, KT):
                    if i in (0, 4) and k >= NCT:
                        wait_y(k, i // 4)
                    last = out_step(i, k)
                last.then_inc(p_out, 1)

        @block.scalar
        def _(act):
            linked = [0]

            def link(ins):
                linked[0] += 1
                ins.then_inc(a_link, 1)
                act.wait_ge(a_link, linked[0])

            act.wait_ge(p_rows, 1)
            act.activation(cols[:, :], pv[:, 0:52], ACT.Copy).then_inc(a_cols, 1)
            act.wait_ge(a_cols, 1)
            act.activation(cact[:, :], cols[:, C_C:C_C + KT], ACT.Tanh, scale=0.5).then_inc(a_cols, 1)

            def sum_x(t):
                act.wait_ge(s_x[t], 16)
                if t:
                    act.wait_ge(a_ssx, t)
                act.activation(junk[:, :], xs[:, t, :], ACT.Square, accum_out=ssx[:, t:t + 1]).then_inc(a_ssx, 1)

            def w_hi(i):
                u, _ = pieces[i]
                r = raw_at["w", i]
                act.wait_ge(s_raw[r % 3], raw_due[r])
                if free[u]:
                    act.wait_ge(p_main, free[u])
                slot, ks = whalf(i)
                act.activation(wts[:, slot, 0, ks, :], raw[:, r % 3, :].rearrange("p (k n) -> p k n", k=4),
                               ACT.Copy).then_inc(a_hi, 1)

            def modulate(idx):
                k = idx % KT
                act.wait_ge(p_xT, idx + 1)
                if idx < KT:
                    act.wait_ge(d_ab, 2 * k + 2)
                if idx >= 2:
                    act.wait_ge(d_hlo, idx - 1)
                act.activation(h32[:, idx % 2, :], tr[:, idx % 2, :], ACT.Identity, scale=modA[:, k:k + 1],
                               bias=modB[:, k:k + 1]).then_inc(a_h32, 1)

            act.wait_ge(g_const, 4)
            sum_x(0)
            sum_x(1)
            sum_x(2)
            sum_x(3)
            act.wait_ge(p_rows, 2)
            act.activation(cw[:, :, :], pv[:, 64:192].rearrange("p (i t) -> p i t", t=32)[:, :, 0:TAPS], ACT.Copy,
                           scale=0.5).then_inc(a_cols, 1)
            for i in range(3):
                w_hi(i)
            modulate(0)
            w_hi(3)
            for k in range(1, KT):
                modulate(k)
            for t in range(4, NT):
                sum_x(t)

            def tanh_g(i, half, src, use):
                act.wait_ge(p_main, use + 1)
                act.activation(z[:, i, PAD + half * HALF:PAD + (half + 1) * HALF], src, ACT.Tanh,
                               scale=0.5).then_inc(a_tanh, 1)

            tanh_g(0, 0, pm[:, 0, :], 0)
            tanh_g(1, 0, pm[:, 1, :], 1)
            for idx in range(KT, 2 * KT):
                modulate(idx)
            w_hi(4)
            w_hi(5)
            tanh_g(0, 1, ps[:, 1, :], 4)
            tanh_g(1, 1, pm[:, 0, :], 6)
            for i in range(6, 10):
                w_hi(i)
            for i, use in ((2, 8), (3, 12)):
                for half in range(2):
                    tanh_g(i, half, pm[:, (use + half - 6) % 3, :], use + half)
            for i in range(10, 14):
                w_hi(i)

            def bank(i):
                return pm[:, (i - 6) % 3, :]

            def squares_v(t):
                act.wait_ge(p_main, 16 + 2 * t + 2)
                if t:
                    act.wait_ge(g_rope, t)
                    act.wait_ge(d_ss, t)
                if t >= 5:
                    act.wait_ge(p_PV, 2 * (t - 4) + 2)
                act.activation(rot2[:, 0:512], bank(16 + 2 * t), ACT.Square)
                act.activation(rot2[:, 512:640], bank(17 + 2 * t)[:, 0:P], ACT.Square)
                act.activation(qk[:, 0:512], bank(16 + 2 * t), ACT.Copy)
                act.activation(qk[:, 512:640], bank(17 + 2 * t)[:, 0:P], ACT.Copy)
                act.activation(v[:, t % 5, :], bank(17 + 2 * t)[:, P:2 * P], ACT.Copy, scale=0.5).then_inc(a_v, 1)

            def copy_pt(b, g):
                act.wait_ge(p_PT, 2 * b + g + 1)
                if b:
                    act.wait_ge(p_PV, 2 * b + g - 1)
                act.activation(pcur[g][:, :, :], tr[:, g, :].rearrange("p (j n) -> p j n", j=GRP), ACT.Copy).then_inc(a_pt, 1)

            def exps(b, part):
                s = sel1 if b % 2 else sel0
                if part == 0:
                    act.wait_ge(d_nmx, b + 1)
                    if b:
                        act.wait_ge(d_rden, b)
                for i in range(4 * part, 4 * part + 4):
                    act.activation(s[:, i, :], s[:, i, :], ACT.Exp, bias=nmx[:, b % 2, i:i + 1],
                                   accum_out=psum_p[:, i:i + 1])
                if part == 1:
                    act.activation(esink[:, :], sdiff[:, :], ACT.Exp).then_inc(a_exp, 1)

            def copy_qk(b):
                act.wait_ge(p_T, b + 1)
                if b:
                    act.wait_ge(p_S, 2 * b)
                act.activation(qT[:, :, :], tr[:, 0, :].rearrange("p (j n) -> p j n", j=GRP), ACT.Copy)
                act.activation(kT[:, b % 2, :], tr[:, 1, 0:P], ACT.Copy).then_inc(a_qT, 1)

            def copy_scores(b, jj):
                s = sel1 if b % 2 else sel0
                act.wait_ge(p_S, 2 * b + jj + 1)
                if b >= 2 and jj == 0:
                    act.wait_ge(p_PT, 2 * (b - 2) + 2)
                src = ps[:, :, :].rearrange("p g (j s n) -> p (g j) s n", j=2, s=2)[:, :, b % 2, :]
                act.activation(s[:, 4 * jj:4 * jj + 4, :], src, ACT.Copy).then_inc(a_sel, 1)

            def normalize(b):
                s = sel1 if b % 2 else sel0
                act.wait_ge(d_rden, b + 1)
                for i in range(NH):
                    last = act.activation(s[:, i, :], s[:, i, :], ACT.Copy, scale=rden[:, i:i + 1])
                last.then_inc(a_pn, 1)

            def copy_att(b):
                act.wait_ge(p_PV, 2 * b + 2)
                act.activation(att[:, :, b * P:(b + 1) * P], pv[:, :].rearrange("p (j n) -> p j n", j=GRP),
                               ACT.Copy).then_inc(a_att, 1)

            def tanh_gate(m, half):
                i = 32 + 2 * m + half
                act.wait_ge(p_main, i + 1)
                if m < NCT:
                    if m == 0:
                        act.wait_ge(d_gcol, 1)
                    if m == 2:
                        act.wait_ge(p_PV, 16)
                    if m == 3:
                        act.wait_ge(p_PT, 16)
                    dst = gb[:, m, half * HALF:(half + 1) * HALF]
                else:
                    if m > NCT:
                        act.wait_ge(d_ya, 2 * (m - NCT - 1) + half + 1)
                    dst = obuf[:, half, :]
                act.activation(dst, bank(i), ACT.Tanh, scale=0.5).then_inc(a_tanh, 1)

            for n in range(16):
                t, b2, b3, b4 = n - 1, n - 2, n - 3, n - 4
                if 0 <= b4 < NT:
                    copy_pt(b4, 0)
                    copy_pt(b4, 1)
                if n > 8 and n != 11:
                    tanh_gate(n - 9, 1)
                if 0 <= t < NT:
                    squares_v(t)
                if 0 <= b3 < NT:
                    exps(b3, 0)
                if 0 <= b2 < NT:
                    copy_qk(b2)
                if 0 <= b3 < NT:
                    exps(b3, 1)
                if 0 <= b2 < NT:
                    copy_scores(b2, 0)
                if 0 <= b4 < NT:
                    copy_att(b4)
                if n == 11:
                    tanh_gate(2, 0)
                    tanh_gate(2, 1)
                if 0 <= b3 < NT:
                    normalize(b3)
                if 0 <= b2 < NT:
                    copy_scores(b2, 1)
                if n == 14:
                    for ct in range(NCT):
                        act.wait_ge(d_dm, ct + 1)
                        if ct == 2:
                            act.wait_ge(p_mean, 1)
                        act.activation(sq[ct], conv_out[ct], ACT.Square).then_inc(a_sq, 1)
                if n == 15:
                    act.wait_ge(p_sq, 1)
                    act.activation(lnA[:, :].rearrange("p (a n) -> p a n", a=2), ps[:, :, :], ACT.Copy).then_inc(a_lv, 1)
                if n >= 8 and n != 10:
                    tanh_gate(n - 8, 0)
                if 7 <= n < 11:
                    w_hi(2 * n)
                    w_hi(2 * n + 1)
                if n == 12:
                    w_hi(22)
                    w_hi(23)
                if n == 13:
                    act.wait_ge(p_gbc, 1)
                    act.wait_ge(p_PV, 16)
                    act.activation(gbc[:, :].rearrange("p (a n) -> p a n", a=2), tr[:, :, :], ACT.Copy).then_inc(a_gbc, 1)
                    w_hi(24)
                    w_hi(25)

            def y_hi(i):
                k, half = y_order[i]
                sl = slice(half * HALF, (half + 1) * HALF)
                if i < 8:
                    act.wait_ge(d_ya, 2 * k + half + 1)
                    act.wait_ge(p_main, 47 + half)
                else:
                    act.wait_ge(d_yb, i - 7)
                act.activation(h[:, 0, k, sl], y_src(k, sl), ACT.Copy).then_inc(a_yhi, 1)

            for i in range(4):
                y_hi(i)
            tanh_gate(7, 1)
            for i in range(4, 8):
                y_hi(i)
            for i in range(8):
                ct, sl = i % NCT, slice((i // NCT) * HALF, (i // NCT + 1) * HALF)
                act.wait_ge(d_e, i + 1)
                if i >= 2:
                    act.wait_ge(d_yb, i - 1)
                act.activation(sq[1 + 2 * (i % 2)][:, 0:HALF], conv_out[ct][:, sl], ACT.Tanh, scale=lnc[:, 0, ct:ct + 1],
                               bias=lnc[:, 1, ct:ct + 1]).then_inc(a_ty, 1)
                if i >= 1:
                    y_hi(8 + i - 1)
            y_hi(15)
            for i in range(26, 30):
                w_hi(i)

        @block.vector
        def _(dve):
            linked = [0]

            def link(ins):
                linked[0] += 1
                ins.then_inc(d_link, 1)
                dve.wait_ge(d_link, linked[0])

            dve.wait_ge(a_cols, 2)
            link(dve.scalar_tensor_tensor(out=cact[:, :], in0=cact[:, :], scalar=1.0, in1=cols[:, C_C:C_C + KT],
                                          op0=ALU.add, op1=ALU.mult))
            dve.tensor_scalar(cact[:, :], cact[:, :], 0.5, None, ALU.mult).then_inc(d_cact, 1)
            dve.tensor_scalar(bs1[:, :], cols[:, C_SC:C_SC + KT], 1.0, None, ALU.add)
            for i, (c0, f) in enumerate(((C_LW, 0.5), (C_LB, 0.5), (C_LW, 0.25), (C_LB, 0.25))):
                last = dve.tensor_scalar(lnc[:, i, :], cols[:, c0:c0 + NCT], f, None, ALU.mult)
            last.then_inc(d_cact, 1)

            def normalize_x(t):
                dve.tensor_scalar(xs[:, t, :], xs[:, t, :], rsx[:, t:t + 1], None, ALU.mult).then_inc(d_xn, 1)

            def ada_sums(k):
                if k == 0:
                    dve.wait_ge(d_cact, 2)
                dve.wait_ge(s_slab[k % 3], 32 * (k // 3 + 1))
                if k >= 2:
                    dve.wait_ge(p_ada, k - 1)
                for i in range(3):
                    for ch in range(2):
                        ct = 3 * ch + i
                        acc = ada_acc[:, k % 2, ch, :]
                        src = slab[:, k % 3, ct, :, :].rearrange("p a n -> p (a n)")
                        if i == 0:
                            ins = dve.tensor_scalar(acc, src, cact[:, ct:ct + 1], None, ALU.mult)
                        else:
                            dve.wait_ge(d_ada, 6 * k + 2 * i + ch - 1)
                            ins = dve.scalar_tensor_tensor(out=acc, in0=src, scalar=cact[:, ct:ct + 1], in1=acc,
                                                           op0=ALU.mult, op1=ALU.add)
                        ins.then_inc(d_ada, 1)

            def ada_finish(k):
                dve.wait_ge(p_ada, k + 1)
                b = pv if k % 2 == 0 else ps[:, 1, :]
                dve.scalar_tensor_tensor(out=modA[:, k:k + 1], in0=b[:, 1:2], scalar=bs1[:, k:k + 1],
                                         in1=cols[:, C_NW + k:C_NW + k + 1], op0=ALU.add, op1=ALU.mult).then_inc(d_ab, 1)
                dve.tensor_tensor(modB[:, k:k + 1], b[:, 0:1], cols[:, C_SH + k:C_SH + k + 1], ALU.add).then_inc(d_ab, 1)

            def split_h(idx):
                half, k = idx // KT, idx % KT
                sl = slice(half * HALF, (half + 1) * HALF)
                dve.wait_ge(a_h32, idx + 1)
                dve.tensor_copy(h[:, 0, k, sl], h32[:, idx % 2, :]).then_inc(d_hhi, 1)
                dve.wait_ge(d_hhi, idx + 1)
                dve.tensor_tensor(h[:, 1, k, sl], h32[:, idx % 2, :], h[:, 0, k, sl].bitcast(F32),
                                  ALU.subtract).then_inc(d_hlo, 1)

            dve.wait_ge(g_rsx, 1)
            for t in range(4):
                normalize_x(t)
            ada_sums(0)
            ada_finish(0)
            for k in range(KT):
                if k + 1 < KT:
                    ada_sums(k + 1)
                split_h(k)
                if k + 1 < KT:
                    ada_finish(k + 1)
            dve.wait_ge(g_rsx, 2)
            for t in range(4, NT):
                normalize_x(t)
            for idx in range(KT, 2 * KT):
                split_h(idx)
            dve.wait_ge(p_ada, KT)
            dve.memset(z[:, :, 0:PAD], 0.0).then_inc(d_link, 1)
            linked[0] += 1

            def glu(i, half, src, use, n_tanh):
                dve.wait_ge(p_main, use + 1)
                dve.wait_ge(a_tanh, n_tanh)
                sl = slice(PAD + half * HALF, PAD + (half + 1) * HALF)
                dve.scalar_tensor_tensor(out=z[:, i, sl], in0=z[:, i, sl], scalar=1.0, in1=src,
                                         op0=ALU.add, op1=ALU.mult).then_inc(d_glu, 1)

            done = [0]

            def conv(n):
                for s in range(done[0], done[0] + n):
                    g, j = s // TAPS, s % TAPS
                    if j == 0:
                        dve.wait_ge(d_link, linked[0])
                        dve.wait_ge(d_glu, 4 * g + 4)
                        if g == 1:
                            dve.wait_ge(d_conv, 2 * TAPS)
                    for e in range(2):
                        i = 2 * g + e
                        acc = cacc[:, e, :] if g == 0 else z[:, e, 0:S]
                        src = z[:, i, j:j + S]
                        if j == 0:
                            ins = dve.tensor_scalar(acc, src, cw[:, i, 0:1], cols[:, C_CB + i:C_CB + i + 1],
                                                    ALU.mult, ALU.add)
                        else:
                            dve.wait_ge(d_conv, 2 * s + e - 1)
                            ins = dve.scalar_tensor_tensor(out=acc, in0=src, scalar=cw[:, i, j:j + 1], in1=acc,
                                                           op0=ALU.mult, op1=ALU.add)
                        ins.then_inc(d_conv, 1)
                done[0] += n

            dve.wait_ge(a_cols, 3)
            glu(0, 0, pm[:, 2, :], 2, 1)
            glu(1, 0, ps[:, 0, :], 3, 2)
            glu(0, 1, pv[:, :], 5, 3)
            glu(1, 1, pm[:, 1, :], 7, 4)

            def gate_sum(i):
                r = raw_at["g", i]
                dve.wait_ge(s_raw[r % 3], raw_due[r])
                if i == 0:
                    dve.wait_ge(p_xT, 16)
                    ins = dve.tensor_scalar(gacc[:, :], raw[:, r % 3, :], cact[:, i:i + 1], None, ALU.mult)
                else:
                    dve.wait_ge(d_gp, i)
                    ins = dve.scalar_tensor_tensor(out=gacc[:, :], in0=raw[:, r % 3, :], scalar=cact[:, i:i + 1],
                                                   in1=gacc[:, :], op0=ALU.mult, op1=ALU.add)
                ins.then_inc(d_gp, 1)

            conv(2)
            for i in range(4):
                gate_sum(i)
                conv(1)
            glu(2, 0, pm[:, (10 - 6) % 3, :], 10, 5)
            conv(1)
            gate_sum(4)
            glu(2, 1, pm[:, (11 - 6) % 3, :], 11, 6)
            for i in range(5, 8):
                conv(1)
                gate_sum(i)
            conv(1)
            glu(3, 0, pm[:, (14 - 6) % 3, :], 14, 7)
            conv(2)
            glu(3, 1, pm[:, (15 - 6) % 3, :], 15, 8)
            dve.wait_ge(p_gcol, 1)
            dve.tensor_tensor(gcol[:, :], tr[:, 0, 0:KT], cols[:, C_GT:C_GT + KT], ALU.add).then_inc(d_gcol, 1)

            def bank(i):
                return pm[:, (i - 6) % 3, :]

            def sum_squares(t):
                dve.wait_ge(a_v, t + 1)
                if t:
                    dve.wait_ge(g_rs, t)
                dve.tensor_reduce(ssq[:, :], rot2[:, :].rearrange("p (h d) -> p h d", d=DH), AX.X, ALU.add).then_inc(d_ss, 1)

            def normalize_qk(t):
                dve.wait_ge(g_rs, t + 1)
                heads = qk[:, :].rearrange("p (h d) -> p h d", d=DH)
                dve.tensor_tensor(heads, heads, rsq[:, :].unsqueeze(2).to_broadcast([P, NH + NKV, DH]),
                                  ALU.mult).then_inc(d_qn, 1)

            def previous_keys(b, jj):
                s = sel1 if b % 2 else sel0
                dve.wait_ge(a_sel, 2 * b + jj + 1)
                src = ps[:, :, :].rearrange("p g (j s n) -> p (g j) s n", j=2, s=2)[:, :, 1 - b % 2, :]
                dve.copy_predicated(s[:, 4 * jj:4 * jj + 4, :], later[:, :].unsqueeze(1).to_broadcast([P, 4, P]),
                                    src).then_inc(d_cp, 1)

            def row_max(b):
                s = sel1 if b % 2 else sel0
                if b == 0:
                    dve.wait_ge(g_blk0, 1)
                else:
                    dve.wait_ge(d_cp, 2 * b)
                if b:
                    dve.wait_ge(a_exp, b)
                link(dve.tensor_reduce(nmx[:, b % 2, :], s[:, :, :], AX.X, ALU.max, negate=True))
                m = nmx[:, b % 2, :].rearrange("p (jj g jh) -> p jj g jh", jj=2, g=NKV)
                link(dve.tensor_tensor(m, m, nsnk[:, :].rearrange("p (g jj jh) -> p jj g jh", g=NKV, jj=2), ALU.min))
                dve.tensor_tensor(sdiff[:, :].rearrange("p (jj g jh) -> p jj g jh", jj=2, g=NKV), m,
                                  snk[:, :].rearrange("p (g jj jh) -> p jj g jh", g=NKV, jj=2), ALU.add).then_inc(d_nmx, 1)

            def denominators(b):
                dve.wait_ge(a_exp, b + 1)
                if b:
                    dve.wait_ge(a_pn, b)
                link(dve.tensor_tensor(psum_p[:, :], psum_p[:, :], esink[:, :], ALU.add))
                dve.reciprocal(rden[:, :], psum_p[:, :]).then_inc(d_rden, 1)

            def gate(m, half):
                i = 32 + 2 * m + half
                sl = slice(half * HALF, (half + 1) * HALF)
                dve.wait_ge(a_tanh, 8 + 2 * m + half + 1)
                dst = gb[:, m, sl] if m < NCT else obuf[:, half, :]
                dve.scalar_tensor_tensor(out=dst, in0=dst, scalar=1.0, in1=bank(i), op0=ALU.add,
                                         op1=ALU.mult).then_inc(d_gate, 1)
                if m >= NCT:
                    j = m - NCT
                    dve.wait_ge(d_gate, 2 * m + half + 1)
                    dve.wait_ge(a_att, NT)
                    dve.tensor_tensor(att[:, j, sl], att[:, j, sl], obuf[:, half, :], ALU.mult).then_inc(d_ya, 1)

            def taps(n):
                conv(min(n, 2 * TAPS - done[0]))

            def s23():
                dve.wait_ge(d_conv, 4 * TAPS)
                dve.wait_ge(p_PV, 16)
                dve.tensor_tensor(lnB[:, :], conv_out[2], conv_out[3], ALU.add).then_inc(d_s23, 1)

            def minus_mean():
                dve.wait_ge(p_mean, 1)
                for ct in range(NCT):
                    dve.scalar_tensor_tensor(out=conv_out[ct], in0=ps[:, :, :].rearrange("p a n -> p (a n)"),
                                             scalar=-1.0 / 512, in1=conv_out[ct], op0=ALU.mult,
                                             op1=ALU.add).then_inc(d_dm, 1)

            def variances():
                dve.wait_ge(p_var, 1)
                dve.tensor_copy(ssx[:, :], pv[:, 0:NT]).then_inc(d_var, 1)
                dve.wait_ge(g_rstd, 1)
                dve.tensor_tensor(lnbuf[:, 0, 0:S].rearrange("p (t n) -> p t n", t=NT),
                                  ident[:, :].unsqueeze(1).to_broadcast([P, NT, P]),
                                  rsx[:, :].unsqueeze(2).to_broadcast([P, NT, P]), ALU.mult).then_inc(d_ldiag, 1)

            for n in range(16):
                t, b2, b3 = n - 1, n - 2, n - 3
                if n == 0:
                    taps(3)
                if n >= 13:
                    taps(1)
                if n == 11:
                    gate(2, 0)
                if n > 8:
                    gate(n - 9, 1)
                if 0 <= t < NT:
                    taps(1)
                    sum_squares(t)
                    taps(1)
                    normalize_qk(t)
                taps(1)
                if 0 <= b3 < NT:
                    denominators(b3)
                if 0 <= b2 < NT:
                    if b2:
                        previous_keys(b2, 0)
                    taps(1)
                    if b2:
                        previous_keys(b2, 1)
                    row_max(b2)
                if n >= 10:
                    taps(2)
                if n == 14:
                    minus_mean()
                if n >= 8 and n != 10:
                    gate(n - 8, 0)
                if n == 12:
                    dve.wait_ge(p_PT, 16)
                    dve.wait_ge(g_rope, NT)
                    dve.wait_ge(p_T, NT)
                    dve.tensor_tensor(gdiag[:, :, :], ident[:, :].unsqueeze(1).to_broadcast([P, KT, P]),
                                      gcol[:, :].unsqueeze(2).to_broadcast([P, KT, P]), ALU.mult).then_inc(d_gdiag, 1)
                if n == 13:
                    conv(2 * TAPS - done[0])
                    s23()
            gate(7, 1)
            variances()
            dve.wait_ge(p_bc, 1)

            def normed(i):
                e, sl = conv_out[i % NCT], slice((i // NCT) * HALF, (i // NCT + 1) * HALF)
                dve.tensor_tensor(e[:, sl], e[:, sl], ps[:, i // NCT, :], ALU.mult).then_inc(d_e, 1)

            normed(0)
            for i in range(8):
                ct, sl = i % NCT, slice((i // NCT) * HALF, (i // NCT + 1) * HALF)
                if i < 7:
                    normed(i + 1)
                e, ty = conv_out[ct][:, sl], sq[1 + 2 * (i % 2)][:, 0:HALF]
                dve.wait_ge(a_ty, i + 1)
                link(dve.tensor_scalar(e, e, lnc[:, 2, ct:ct + 1], lnc[:, 3, ct:ct + 1], ALU.mult, ALU.add))
                link(dve.scalar_tensor_tensor(out=ty, in0=ty, scalar=1.0, in1=e, op0=ALU.add, op1=ALU.mult))
                dve.tensor_tensor(gb[:, ct, sl], gb[:, ct, sl], ty, ALU.mult).then_inc(d_yb, 1)

            obanks = [tr[:, 0, :], tr[:, 1, :], pm[:, 0, :], pm[:, 1, :], pm[:, 2, :]]
            for i in range(2 * NT):
                n = i // NT
                dve.wait_ge(p_out, i + 1)
                if i >= 2:
                    dve.wait_ge(g_fin, i - 1)
                dve.tensor_tensor(obuf[:, i % 2, :], obanks[i % 5], gbc[:, n * HALF:(n + 1) * HALF],
                                  ALU.mult).then_inc(d_o, 1)


def rope_table():
    inv = (10000.0 ** (-np.arange(0, DH, 2) / DH)).astype(np.float32)
    ang = np.arange(S, dtype=np.float32)[:, None] * inv[None, :]
    co, si = np.cos(ang), np.sin(ang)
    return np.ascontiguousarray(np.concatenate([co, co, -si, si], axis=1).astype(np.float32))


_INS = ["x", "c", "w_ada", "b_ada", "norm_w", "w_in", "q_norm_w", "k_norm_w", "sinks", "conv_w", "conv_b",
        "ln_w", "ln_b", "w_out"]


def kernel(**inputs):
    import concourse.bacc as bacc
    from concourse.bass_utils import run_bass_kernel_spmd

    nc = bacc.Bacc("TRN2", target_bir_lowering=False, num_devices=1)
    arrays = {f"in_{n}": np.ascontiguousarray(inputs[n]) for n in _INS}
    arrays["in_rope"] = rope_table()
    args = [nc.dram_tensor(n, a.shape, mybir.dt.from_np(a.dtype), kind="ExternalInput").ap() for n, a in arrays.items()]
    args.append(nc.dram_tensor("out_0", (1, S, D), F32, kind="ExternalOutput").ap())
    build(nc, *args)
    return run_bass_kernel_spmd(nc, [arrays], core_ids=[0]).results[0]["out_0"]
```

```python
from contextlib import ExitStack

import numpy as np

import concourse.bass as bass
from concourse import mybir

F32 = mybir.dt.float32
F32R = mybir.dt.float32r
U8 = mybir.dt.uint8
ALU = mybir.AluOpType
ACT = mybir.ActivationFunctionType
AX = mybir.AxisListType

P = 128
D = 1024
S = 1024
HALF = 512
KT = D // P
NT = S // P
DH = 64
NH = 8
NKV = 2
GRP = NH // NKV
TAPS = 31
PAD = TAPS - 1
ZW = S + 32
NCT = 4
EPS = 1e-6
FILL = -1.0e38
U = 256
Q0, K0, GA0, A0, G0, GB0 = 0, 512, 768, 1280, 1792, 2304


def build(nc, x, c, w_ada, b_ada, norm_w, w_in, q_norm_w, k_norm_w, sinks,
          conv_w, conv_b, ln_w, ln_b, w_out, rope_rows, out):
    base = 16512

    def at(name, shape, dtype, offset):
        return nc.alloc_sbuf_tensor_at(name, [P] + shape, dtype, offset=base + offset)

    H_AT, W_AT, RAW_AT, XG_AT, C_AT, S_AT = 0, 65536, 131072, 143360, 176128, 201216
    Z_AT = W_AT
    h = at("h", [2, KT, S], F32R, H_AT)
    wts = at("wts", [4, 2, KT, U], F32R, W_AT)
    sel0 = at("sel0", [NH, P], F32, Z_AT)
    pcur = [at("pcur0", [GRP, P], F32, Z_AT + 4096), at("pcur1", [GRP, P], F32, XG_AT + 24576)]
    pprev = [at("pprev0", [GRP, P], F32, Z_AT + 6144), at("pprev1", [GRP, P], F32, XG_AT + 26624)]
    qk = at("qk", [10 * DH], F32, Z_AT + 8192)
    rot1 = at("rot1", [10 * DH], F32, Z_AT + 10752)
    rot2 = at("rot2", [10 * DH], F32, Z_AT + 13312)
    lnA = at("lnA", [S], F32, Z_AT)
    lnB = at("lnB", [S], F32, Z_AT + 4096)
    vrows = at("vrows", [P], F32, Z_AT)
    cwrows = at("cwrows", [512], F32, Z_AT + 512)
    h32 = at("h32", [2, HALF], F32, Z_AT + 2560)
    junk = at("junk", [D], F32, Z_AT + 6656)
    ada_acc = at("ada_acc", [2, 2, 2 * P], F32, Z_AT + 10752)
    gdiag = at("gdiag", [NT, P], F32, Z_AT + 8192)
    raw = at("raw", [3, 1024], F32, RAW_AT)
    xs = at("xs", [NT, D], F32, XG_AT)
    att = at("att", [NCT, S], F32, XG_AT)
    gb = at("gb", [NCT, S], F32, XG_AT + 16384)
    gacc = at("gacc", [D], F32, XG_AT + 16384)
    sel1 = at("sel1", [NH, P], F32, XG_AT + 16384 + 12288)
    xr = at("xr", [NT, D], F32, XG_AT)
    z = at("z", [NCT, ZW], F32, C_AT)
    cacc = at("cacc", [2, S], F32, C_AT + 4 * 4 * ZW)
    slab = at("slab", [3, KT, 2, P], F32, C_AT)
    lnbuf = at("lnbuf", [2, ZW], F32, C_AT + 2 * 4 * ZW)
    v = at("v", [5, P], F32, S_AT)
    qT = at("qT", [GRP, P], F32, S_AT + 2560)
    kT = at("kT", [2, P], F32, S_AT + 4608)
    ropr = at("ropr", [P], F32, S_AT + 5632)
    tab = at("tab", [2, 2, NKV, DH], F32, S_AT + 6144)
    gbc = at("gbc", [D], F32, S_AT)
    obuf = at("obuf", [2, HALF], F32, S_AT + 4096)
    spot = [S_AT + 8192]

    def small(name, shape, dtype=F32):
        t = at(name, shape, dtype, spot[0])
        n = int(np.prod(shape)) * (1 if dtype == U8 else 4)
        spot[0] += -(-n // 32) * 32
        return t

    ident = small("ident", [P])
    ones = small("ones", [P])
    later = small("later", [P], U8)
    cols = small("cols", [52])
    cw = small("cw", [NCT, TAPS])
    wqk = small("wqk", [NKV, DH])
    snk = small("snk", [NH])
    nsnk = small("nsnk", [NH])
    mhalf = small("mhalf", [10])
    cact = small("cact", [KT])
    tiny = small("tiny", [12])
    ssx = small("ssx", [NT])
    rsx = small("rsx", [NT])
    ssq = small("ssq", [10])
    rsq = small("rsq", [10])
    modA = small("modA", [KT])
    modB = small("modB", [KT])
    bs1 = small("bs1", [KT])
    gcol = small("gcol", [KT])
    nmx = small("nmx", [2, NH])
    sdiff = small("sdiff", [NH])
    esink = small("esink", [NH])
    psum_p = small("psum_p", [NH])
    rden = small("rden", [NH])
    lnc = small("lnc", [4, NCT])
    assert spot[0] <= 229344 - base, spot[0]
    C_C, C_NW, C_SH, C_SC, C_GT, C_CB, C_LW, C_LB = 0, 8, 16, 24, 32, 40, 44, 48

    with ExitStack() as ctx:
        def psum(name, shape):
            return ctx.enter_context(nc.psum_tensor(name, [P] + shape, F32))

        def sem(name):
            return ctx.enter_context(nc.semaphore(name))

        pm = psum("pm", [3, HALF])
        ps = psum("ps", [2, HALF])
        tr = psum("tr", [2, HALF])
        pv = psum("pv", [HALF])

        s_vec, s_cw, s_bc = sem("s_vec"), sem("s_cw"), sem("s_bc")
        s_x = [sem(f"s_x{t}") for t in range(NT)]
        s_slab = [sem(f"s_slab{i}") for i in range(3)]
        s_raw = [sem(f"s_raw{i}") for i in range(3)]
        s_rope = sem("s_rope")
        s_xr = [sem(f"s_xr{t}") for t in range(NT)]
        s_out = sem("s_out")
        g_const, g_rsx, g_lo, g_tab = sem("g_const"), sem("g_rsx"), sem("g_lo"), sem("g_tab")
        g_rs, g_mask, g_rope = sem("g_rs"), sem("g_mask"), sem("g_rope")
        g_blk0, g_ylo, g_fin, g_link = sem("g_blk0"), sem("g_ylo"), sem("g_fin"), sem("g_link")
        g_s01, g_rstd, g_gp = sem("g_s01"), sem("g_rstd"), sem("g_gp")
        p_rows, p_xT, p_ada, p_main = sem("p_rows"), sem("p_xT"), sem("p_ada"), sem("p_main")
        p_gcol, p_gbc, p_T, p_S, p_PT, p_PV = sem("p_gcol"), sem("p_gbc"), sem("p_T"), sem("p_S"), sem("p_PT"), sem("p_PV")
        p_mean, p_sq, p_var, p_bc, p_out = sem("p_mean"), sem("p_sq"), sem("p_var"), sem("p_bc"), sem("p_out")
        a_lv, a_gp = sem("a_lv"), sem("a_gp")
        a_cols, a_ssx, a_h32, a_hi, a_tanh = sem("a_cols"), sem("a_ssx"), sem("a_h32"), sem("a_hi"), sem("a_tanh")
        a_v, a_pt, a_exp, a_qT, a_sel = sem("a_v"), sem("a_pt"), sem("a_exp"), sem("a_qT"), sem("a_sel")
        a_pn, a_att, a_yhi, a_gbc, a_sq, a_ty = sem("a_pn"), sem("a_att"), sem("a_yhi"), sem("a_gbc"), sem("a_sq"), sem("a_ty")
        a_link = sem("a_link")
        d_cact, d_xn, d_ada, d_ab, d_hlo = sem("d_cact"), sem("d_xn"), sem("d_ada"), sem("d_ab"), sem("d_hlo")
        d_glu, d_conv, d_gcol, d_ss, d_qn = sem("d_glu"), sem("d_conv"), sem("d_gcol"), sem("d_ss"), sem("d_qn")
        d_cp, d_nmx, d_rden, d_gate, d_ya = sem("d_cp"), sem("d_nmx"), sem("d_rden"), sem("d_gate"), sem("d_ya")
        d_gdiag, d_s23, d_dm, d_var, d_ldiag, d_e, d_v, d_yb, d_o, d_link = (
            sem("d_gdiag"), sem("d_s23"), sem("d_dm"), sem("d_var"), sem("d_ldiag"), sem("d_e"), sem("d_v"),
            sem("d_yb"), sem("d_o"), sem("d_link"))

        units = [(w_in, A0), (w_in, G0), (w_in, G0 + U), (w_in, A0 + U), (w_in, Q0), (w_in, Q0 + U), (w_in, K0),
                 (w_in, GB0), (w_in, GB0 + U), (w_in, GA0), (w_in, GA0 + U),
                 (w_out, U), (w_out, 0), (w_out, 2 * U), (w_out, 3 * U)]
        slots = [1, 2, 3, 1, 2, 3, 1, 2, 3, 1, 2, 3, 1, 0, 2]
        used = [10, 9, 12, 16, 31, 31, 32, 36, 40, 44, 48]
        free = [0, 0, 0, used[0], used[1], used[2], used[3], used[4], used[5], used[6], used[7],
                used[8], used[9], 0, used[10]]
        pieces = [(0, 0), (1, 0), (0, 1), (1, 1)] + [(u, p) for u in range(2, len(units)) for p in range(2)]
        raws = [("w", i) for i in range(6)] + [("g", i) for i in range(KT)] + [("w", i) for i in range(6, len(pieces))]
        raw_at = {key: r for r, key in enumerate(raws)}

        def transfers(u, p):
            src, c0 = units[u]
            if src is w_in:
                return 4 if GA0 <= c0 < A0 else 1
            return 2 if p == 0 else 1

        raw_due = []
        total = [0, 0, 0]
        for r, (kind, i) in enumerate(raws):
            total[r % 3] += 16 * (transfers(*pieces[i]) if kind == "w" else 1)
            raw_due.append(total[r % 3])

        def split_done(u, p=1):
            return pieces.index((u, p)) + 1

        def whalf(i):
            u, p = pieces[i]
            return slots[u], slice(4 * p, 4 * p + 4)

        LAG = 6
        tap_steps = [[(2 * (q // TAPS) + e, q % TAPS) for e, q in enumerate((s, s - LAG)) if 0 <= q < 2 * TAPS]
                     for s in range(2 * TAPS + LAG)]
        tap_order = [tap for step in tap_steps for tap in step]

        y_order = [(k, half) for k0 in (0, NCT) for half in range(2) for k in range(k0, k0 + NCT)]

        def y_src(k, sl):
            return att[:, k, sl] if k < NCT else gb[:, k - NCT, sl]

        conv_out = [cacc[:, 0, :], cacc[:, 1, :], z[:, 0, 0:S], z[:, 1, 0:S]]
        sq = [lnbuf[:, 0, 0:S], lnbuf[:, 1, 0:S], lnA[:, :], lnB[:, :]]

        block = ctx.enter_context(nc.Block())

        @block.sync
        def _(sp):
            k0 = 0
            for vec, n in ((c, 8), (norm_w, 8), (b_ada, 24), (conv_b, 4), (ln_w, 4), (ln_b, 4)):
                sp.dma_start(vrows[k0:k0 + n, :], vec[0].rearrange("(r p) -> r p", p=P)).then_inc(s_vec, 16)
                k0 += n
            for t in range(4):
                sp.dma_start(xs[:, t, :], x[0, t * P:(t + 1) * P, :]).then_inc(s_x[t], 16)

            def load_raw(r):
                kind, i = raws[r]
                if r >= 3:
                    was, n = raws[r - 3]
                    sp.wait_ge(g_lo if was == "w" else g_gp, n + 1)
                dst = raw[:, r % 3, :]
                if kind == "g":
                    sp.dma_start(dst, w_ada[0, i * P:(i + 1) * P, 2 * D:3 * D]).then_inc(s_raw[r % 3], 16)
                    return
                u, p = pieces[i]
                src, c0 = units[u]
                if src is w_out and p == 0:
                    for g in range(NKV):
                        sp.dma_start(raw[g * DH:(g + 1) * DH, r % 3, :].rearrange("p (k n) -> p k n", k=4),
                                     src[0, g * 256:(g + 1) * 256, c0:c0 + U].rearrange("(k p) n -> p k n", p=DH)
                                     ).then_inc(s_raw[r % 3], 16)
                    return
                if transfers(u, p) == 4:
                    for j in range(2):
                        for g in range(NKV):
                            first = GA0 + (4 * g + 2 * ((c0 - GA0) // U) + j) * DH
                            sp.dma_start(dst.rearrange("p (k j g d) -> p k j g d", k=4, j=2, g=NKV)[:, :, j, g, :],
                                         src[0, p * 512:(p + 1) * 512, first:first + DH].rearrange("(k p) d -> p k d", p=P)
                                         ).then_inc(s_raw[r % 3], 16)
                    return
                sp.dma_start(dst.rearrange("p (k n) -> p k n", k=4),
                             src[0, p * 512:(p + 1) * 512, c0:c0 + U].rearrange("(k p) n -> p k n", p=P)
                             ).then_inc(s_raw[r % 3], 16)

            def load_slab(k):
                if k >= 3:
                    sp.wait_ge(p_ada, k - 2)
                for part in range(2):
                    sp.dma_start(slab[:, k % 3, :, part, :],
                                 w_ada[0, :, part * D + k * P:part * D + (k + 1) * P].rearrange("(t p) n -> p t n", p=P)
                                 ).then_inc(s_slab[k % 3], 16)

            load_slab(0)
            sp.dma_start(cwrows[0:TAPS, :], conv_w[0]).then_inc(s_cw, 16)
            load_raw(0)
            load_raw(1)
            load_slab(1)
            load_raw(2)
            load_slab(2)
            load_raw(3)
            sp.dma_start(wqk[:, 0, :], q_norm_w.to_broadcast([P, DH])).then_inc(s_bc, 16)
            sp.dma_start(wqk[:, 1, :], k_norm_w.to_broadcast([P, DH])).then_inc(s_bc, 16)
            sp.dma_start(snk[:, :], sinks.to_broadcast([P, NH])).then_inc(s_bc, 16)
            for k in range(3, KT):
                load_slab(k)
                if k == 3:
                    load_raw(4)
                else:
                    t = k
                    sp.dma_start(xs[:, t, :], x[0, t * P:(t + 1) * P, :]).then_inc(s_x[t], 16)
                if k == 5:
                    load_raw(5)

            def load_rope(t):
                if t:
                    sp.wait_ge(g_tab, t)
                sp.dma_start(ropr[:, :], rope_rows[t * P:(t + 1) * P, :]).then_inc(s_rope, 16)

            r = 6
            while raws[r] != ("w", 12):
                load_raw(r)
                r += 1
            load_rope(0)
            load_raw(r)
            load_raw(r + 1)
            r += 2
            for t in range(1, NT):
                load_rope(t)
            while r < len(raws):
                load_raw(r)
                r += 1
                if raws[r - 1] == ("w", 28):
                    for t in range(NT):
                        sp.wait_ge(g_ylo, 4 + t % 4 + 1 + (8 if t >= 4 else 0))
                        sp.dma_start(xr[:, t, :], x[0, t * P:(t + 1) * P, :]).then_inc(s_xr[t], 16)
            for i in range(2 * NT):
                sp.wait_ge(g_fin, i + 1)
                t, n = i % NT, i // NT
                sp.dma_start(out[0, t * P:(t + 1) * P, n * HALF:(n + 1) * HALF],
                             xr[:, t, n * HALF:(n + 1) * HALF]).then_inc(s_out, 16)
            sp.wait_ge(s_out, 16 * 2 * NT)

        @block.gpsimd
        def _(gp):
            linked = [0]

            def link(ins):
                linked[0] += 1
                ins.then_inc(g_link, 1)
                gp.wait_ge(g_link, linked[0])

            gp.memset(ones[:, :], 1.0).then_inc(g_const, 1)
            gp.memset(mhalf[:, :], -0.5).then_inc(g_const, 1)
            gp.wait_ge(g_const, 2)
            gp.affine_select(out=ident[:, :], in_=ones[:, :], compare_op=ALU.is_equal, fill=0.0,
                             base=0, pattern=[[-1, P]], channel_multiplier=1).then_inc(g_const, 1)
            link(gp.affine_select(out=junk[:, 0:P], in_=ones[:, :], compare_op=ALU.is_gt, fill=0.0,
                                  base=0, pattern=[[1, P]], channel_multiplier=-1))
            gp.tensor_copy(later[:, :], junk[:, 0:P]).then_inc(g_const, 1)

            def rms_x(half):
                gp.wait_ge(a_ssx, 4 * half + 4)
                sl = slice(4 * half, 4 * half + 4)
                link(gp.tensor_scalar(tiny[:, 0:4], ssx[:, sl], 1.0 / D, EPS, ALU.mult, ALU.add))
                gp.tensor_tensor(rsx[:, sl], tiny[:, 0:4], mhalf[:, 0:4], ALU.pow).then_inc(g_rsx, 1)

            def w_lo(i):
                gp.wait_ge(a_hi, i + 1)
                slot, ks = whalf(i)
                gp.tensor_tensor(wts[:, slot, 1, ks, :],
                                 raw[:, raw_at["w", i] % 3, :].rearrange("p (k n) -> p k n", k=4),
                                 wts[:, slot, 0, ks, :].bitcast(F32), ALU.subtract).then_inc(g_lo, 1)

            rms_x(0)
            for i in range(4):
                w_lo(i)
            gp.wait_ge(s_bc, 48)
            link(gp.tensor_scalar(wqk[:, 0, :], wqk[:, 0, :], DH ** -0.5, None, ALU.mult))
            link(gp.tensor_scalar(nsnk[:, :], snk[:, :], -1.0, None, ALU.mult))
            w_lo(4)
            w_lo(5)
            rms_x(1)
            for i in range(1, KT):
                gp.wait_ge(a_gp, i + 1)
                if i > 1:
                    gp.wait_ge(g_gp, i)
                ins = gp.tensor_tensor(gacc[:, :], gacc[:, :], raw[:, raw_at["g", i] % 3, :], ALU.add)
                ins.then_inc(g_gp, 1 + (i == 1))
            for i in range(6, 10):
                w_lo(i)

            def tables(t):
                gp.wait_ge(s_rope, 16 * (t + 1))
                if t >= 2:
                    gp.wait_ge(g_rope, t - 1)
                cc = ropr[:, 0:DH].unsqueeze(1).to_broadcast([P, NKV, DH])
                gp.tensor_tensor(tab[:, t % 2, 0, :, :], cc, wqk[:, :, :], ALU.mult)
                for lo, other in ((0, 32), (32, 0)):
                    ss = ropr[:, DH + lo:DH + lo + 32].unsqueeze(1).to_broadcast([P, NKV, 32])
                    last = gp.tensor_tensor(tab[:, t % 2, 1, :, lo:lo + 32], ss, wqk[:, :, other:other + 32], ALU.mult)
                last.then_inc(g_tab, 1)

            def rms_qk(t):
                gp.wait_ge(d_ss, t + 1)
                if t:
                    gp.wait_ge(d_qn, t)
                link(gp.tensor_scalar(tiny[:, 0:10], ssq[:, :], 1.0 / DH, EPS, ALU.mult, ALU.add))
                gp.tensor_tensor(rsq[:, :], tiny[:, 0:10], mhalf[:, :], ALU.pow).then_inc(g_rs, 1)

            def rope(t):
                gp.wait_ge(d_qn, t + 1)
                gp.wait_ge(g_tab, t + 1)
                if t:
                    gp.wait_ge(p_T, t)
                q, k = slice(0, 512), slice(512, 640)
                for i, part, grp, n in ((0, q, NKV, GRP), (1, k, 1, NKV)):
                    src = qk[:, part].rearrange("p (g j d) -> p g j d", g=grp, d=DH)
                    r1 = rot1[:, part].rearrange("p (j g d) -> p g j d", g=grp, d=DH)
                    r2 = rot2[:, part].rearrange("p (j g d) -> p g j d", g=grp, d=DH)
                    co = tab[:, t % 2, 0, i, :].unsqueeze(1).unsqueeze(1).to_broadcast([P, grp, n, DH])
                    gp.tensor_tensor(r1, src, co, ALU.mult)
                    for lo, other in ((0, 32), (32, 0)):
                        si = tab[:, t % 2, 1, i, lo:lo + 32].unsqueeze(1).unsqueeze(1).to_broadcast([P, grp, n, 32])
                        last = gp.tensor_tensor(r2[:, :, :, lo:lo + 32], src[:, :, :, other:other + 32], si, ALU.mult)
                link(last)
                gp.tensor_tensor(rot1[:, :], rot1[:, :], rot2[:, :], ALU.add).then_inc(g_rope, 1)

            def masks(b, g):
                gp.wait_ge(a_pt, 2 * b + g + 1)
                if b:
                    gp.affine_select(out=pprev[g][:, :, :], in_=pcur[g][:, :, :], compare_op=ALU.is_gt, fill=0.0,
                                     base=0, pattern=[[0, GRP], [-1, P]], channel_multiplier=1).then_inc(g_link, 1)
                    linked[0] += 1
                    gp.wait_ge(g_link, linked[0])
                gp.affine_select(out=pcur[g][:, :, :], in_=pcur[g][:, :, :], compare_op=ALU.is_ge, fill=0.0,
                                 base=0, pattern=[[0, GRP], [1, P]], channel_multiplier=-1).then_inc(g_mask, 1)

            tables(0)
            for i in range(10, 14):
                w_lo(i)
            for n in range(12):
                b2, b4, t = n - 2, n - 4, n - 1
                if 0 <= b4 < NT:
                    masks(b4, 0)
                    masks(b4, 1)
                if 9 <= n:
                    w_lo(2 * n - 1)
                if 0 <= t < NT:
                    rms_qk(t)
                    rope(t)
                if b2 == 0:
                    gp.wait_ge(a_sel, 2)
                    gp.affine_select(out=sel0[:, :, :], in_=sel0[:, :, :], compare_op=ALU.is_ge, fill=FILL,
                                     base=0, pattern=[[0, NH], [-1, P]], channel_multiplier=1).then_inc(g_blk0, 1)
                if n + 1 < NT:
                    tables(n + 1)
                if 7 <= n < 11:
                    w_lo(2 * n)
                if n == 7:
                    w_lo(15)
            gp.wait_ge(d_conv, tap_order.index((1, TAPS - 1)) + 1)
            gp.wait_ge(p_PV, 16)
            gp.tensor_tensor(lnA[:, :], cacc[:, 0, :], cacc[:, 1, :], ALU.add).then_inc(g_s01, 1)
            for i in range(22, 26):
                w_lo(i)
            def y_lo(i):
                k, half = y_order[i]
                gp.wait_ge(a_yhi, i + 1)
                sl = slice(half * HALF, (half + 1) * HALF)
                gp.tensor_tensor(h[:, 1, k, sl], y_src(k, sl), h[:, 0, k, sl].bitcast(F32),
                                 ALU.subtract).then_inc(g_ylo, 1)

            y_lo(0)
            y_lo(1)
            gp.wait_ge(d_var, 1)
            link(gp.tensor_scalar(tiny[:, 0:8], ssx[:, :], 1.0 / (512 * 32), EPS, ALU.mult, ALU.add))
            gp.tensor_tensor(rsx[:, :], tiny[:, 0:8], mhalf[:, 0:8], ALU.pow).then_inc(g_rstd, 1)
            for i in range(2, 16):
                y_lo(i)
            for i in range(26, 30):
                w_lo(i)

            for i in range(2 * NT):
                gp.wait_ge(d_o, i + 1)
                t, n = i % NT, i // NT
                gp.wait_ge(s_xr[t], 16)
                sl = slice(n * HALF, (n + 1) * HALF)
                gp.tensor_tensor(xr[:, t, sl], xr[:, t, sl], obuf[:, i % 2, :], ALU.add).then_inc(g_fin, 1)

        @block.tensor
        def _(pe):
            pe.wait_ge(g_const, 4)
            pe.wait_ge(s_vec, 96)
            pe.transpose(pv[:, 0:52], vrows[0:52, :], ident[0:52, 0:52]).then_inc(p_rows, 1)

            def x_transposes(idx):
                half, k = idx // KT, idx % KT
                if k == 0:
                    pe.wait_ge(d_xn, 4 * half + 4)
                if idx >= 2:
                    pe.wait_ge(a_h32, idx - 1)
                for t in range(4):
                    last = pe.transpose(tr[:, k % 2, t * P:(t + 1) * P], xs[:, 4 * half + t, k * P:(k + 1) * P], ident[:, :])
                last.then_inc(p_xT, 1)

            def ada_bank(k):
                return pv if k % 2 == 0 else ps[:, 1, :]

            def ada_cols(k):
                if k == 0:
                    pe.wait_ge(d_cact, 1)
                    pe.wait_ge(a_cols, 3)
                if k >= 2:
                    pe.wait_ge(d_ab, 2 * (k - 1))
                pe.wait_ge(s_slab[k % 3], 32 * (k // 3 + 1))
                pe.wait_ge(d_ada, 8 * k + 8)
                for part in range(2):
                    o = ada_bank(k)[:, part:part + 1]
                    pe.matmul(o, slab[:, k % 3, 7, part, :], cact[:, 7:8], start=True, stop=False)
                    last = pe.matmul(o, ada_acc[:, k % 2, 0, part * P:(part + 1) * P], ones[:, 0:1], start=False, stop=True)
                last.then_inc(p_ada, 1)

            def three(out, hi_w, lo_w, hi_x, lo_x, first, last):
                pe.matmul(out, hi_w, hi_x, start=first, stop=False)
                pe.matmul(out, lo_w, hi_x, start=False, stop=False)
                return pe.matmul(out, hi_w, lo_x, start=False, stop=last)

            def channel_step(out, slot, col, half, k):
                sl = slice(half * HALF, (half + 1) * HALF)
                return three(out, wts[:, slot + 1, 0, k, col:col + P], wts[:, slot + 1, 1, k, col:col + P],
                             h[:, 0, k, sl], h[:, 1, k, sl], k == 0, k == KT - 1)

            x_transposes(0)
            pe.wait_ge(s_cw, 16)
            pe.wait_ge(a_cols, 1)
            for i in range(NCT):
                last = pe.transpose(pv[:, 64 + 32 * i:64 + 32 * i + TAPS], cwrows[0:TAPS, i * P:(i + 1) * P],
                                    ident[0:TAPS, 0:TAPS])
            last.then_inc(p_rows, 1)
            ada_cols(0)
            early = [(pm[:, 0, :], 1, 0), (pm[:, 1, :], 1, P), (pm[:, 2, :], 0, 0), (ps[:, 0, :], 0, P)]
            for k in range(KT):
                if k + 1 < KT:
                    x_transposes(k + 1)
                    ada_cols(k + 1)
                pe.wait_ge(d_hlo, k + 1)
                if k % 4 == 0:
                    pe.wait_ge(g_lo, 2 if k == 0 else 4)
                for bank, slot, col in early:
                    last = channel_step(bank, slot, col, 0, k)
                    if k == KT - 1:
                        last.then_inc(p_main, 1)

            def channel_tile(i, out, slot, col, half, each=None):
                for k in range(KT):
                    if each:
                        each(k)
                    if i == 6:
                        pe.wait_ge(d_hlo, KT + k + 1)
                    last = channel_step(out, slot, col, half, k)
                last.then_inc(p_main, 1)

            pe.wait_ge(d_ab, 16)
            pe.wait_ge(g_lo, split_done(2))
            channel_tile(4, ps[:, 1, :], 2, 0, 0)
            channel_tile(5, pv[:, :], 2, P, 0, each=lambda k: x_transposes(KT + k))
            pe.wait_ge(a_tanh, 1)
            channel_tile(6, pm[:, 0, :], 1, 0, 1)
            pe.wait_ge(a_tanh, 2)
            channel_tile(7, pm[:, 1, :], 0, 0, 1)
            pe.wait_ge(d_glu, 1)
            channel_tile(8, pm[:, 2, :], 1, P, 1)
            pe.wait_ge(d_glu, 2)
            channel_tile(9, ps[:, 0, :], 0, P, 1)

            def bank(i):
                return pm[:, (i - 10) % 3, :]

            def wait_bank(i):
                j = i - 3
                if j < 16:
                    sem_, value = {10: (a_tanh, 7), 11: (a_tanh, 8), 12: (d_glu, 5), 13: (d_glu, 6),
                                   14: (d_glu, 7), 15: (d_glu, 8)}[j]
                    pe.wait_ge(sem_, value)
                elif j < 32:
                    pe.wait_ge(a_v, (j - 16) // 2 + 1)
                else:
                    pe.wait_ge(d_gate, j - 31)

            pe.wait_ge(a_tanh, 5)
            channel_tile(10, bank(10), 2, 0, 1)
            pe.wait_ge(d_glu, 3)
            channel_tile(11, bank(11), 2, P, 1)
            pe.wait_ge(g_lo, split_done(3))
            for i in range(12, 16):
                if i == 12:
                    pe.wait_ge(a_tanh, 6)
                else:
                    wait_bank(i)
                channel_tile(i, bank(i), 0, (i - 12) // 2 * P, i % 2)
            pe.wait_ge(g_gp, KT)
            pe.wait_ge(a_h32, 16)
            for i in range(KT):
                last = pe.matmul(tr[:, 0, i:i + 1], gacc[:, i * P:(i + 1) * P], ones[:, 0:1], start=True, stop=True)
            last.then_inc(p_gcol, 1)

            def transpose_qk(b):
                pe.wait_ge(g_rope, b + 1)
                if b == 0:
                    pe.wait_ge(d_gcol, 1)
                else:
                    pe.wait_ge(a_qT, b)
                if b >= 2:
                    pe.wait_ge(a_pt, 2 * (b - 1))
                for j in range(GRP):
                    pe.transpose(tr[:, 0, j * P:(j + 1) * P], rot1[:, j * P:(j + 1) * P], ident[:, :])
                pe.transpose(tr[:, 1, 0:P], rot1[:, 512:640], ident[:, :]).then_inc(p_T, 1)

            def scores(b, jj):
                pe.wait_ge(a_qT, b + 1)
                if b == 0 and jj == 0:
                    pe.wait_ge(d_glu, 4)
                    pe.wait_ge(a_tanh, 3)
                if 2 * b + jj:
                    pe.wait_ge(a_sel, 2 * b + jj)
                if 2 * (b - 1) + jj > 0:
                    pe.wait_ge(d_cp, 2 * (b - 1) + jj)
                for jh in range(2):
                    for g in range(NKV):
                        lhs = qT[g * DH:(g + 1) * DH, 2 * jj + jh, :]
                        if b:
                            o, rhs = ps[:, g, jh * 256:(jh + 1) * 256], kT[g * DH:(g + 1) * DH, :, :]
                        else:
                            o, rhs = ps[:, g, jh * 256:jh * 256 + P], kT[g * DH:(g + 1) * DH, 0, :]
                        last = pe.matmul(o, lhs, rhs, start=True, stop=True)
                last.then_inc(p_S, 1)

            def transpose_p(b):
                pe.wait_ge(a_pn, b + 1)
                pe.wait_ge(a_qT, min(b + 2, NT))
                if b:
                    pe.wait_ge(a_pt, 2 * b)
                s = sel1 if b % 2 else sel0
                for g in range(NKV):
                    for j in range(GRP):
                        last = pe.transpose(tr[:, g, j * P:(j + 1) * P], s[:, (j // 2) * 4 + g * 2 + j % 2, :], ident[:, :])
                    last.then_inc(p_PT, 1)

            def times_v(b, g):
                pe.wait_ge(g_mask, 2 * b + g + 1)
                pe.wait_ge(a_v, b + 1)
                if b:
                    pe.wait_ge(a_att, b)
                else:
                    pe.wait_ge(a_tanh, 4)
                o = pv[g * DH:(g + 1) * DH, :]
                last = pe.matmul(o, v[:, b % 5, g * DH:(g + 1) * DH], pcur[g][:, :, :], start=True, stop=(b == 0))
                if b:
                    last = pe.matmul(o, v[:, (b - 1) % 5, g * DH:(g + 1) * DH], pprev[g][:, :, :], start=False, stop=True)
                last.then_inc(p_PV, 1)

            def attention_step(n, s):
                new, old = n - 2, n - 4
                if 0 <= old < NT:
                    if s == 0:
                        transpose_p(old)
                    if s == 4:
                        times_v(old, 0)
                    if s == 6:
                        times_v(old, 1)
                if 0 <= new < NT:
                    if s == 5:
                        transpose_qk(new)
                    if s == 8:
                        scores(new, 0)
                    if s == 12:
                        scores(new, 1)

            pe.wait_ge(g_lo, split_done(5))
            for t in range(NT):
                ts = slice(t * P, (t + 1) * P)
                for part in range(2):
                    i = 16 + 2 * t + part
                    for k in range(KT):
                        if t == 0 and part == 1 and k % 4 == 0:
                            pe.wait_ge(g_lo, split_done(6, k // 4))
                        attention_step(t, part * KT + k)
                        if k == 0:
                            wait_bank(i)
                        if part == 0:
                            o = bank(i).rearrange("p (s n) -> p s n", s=2)
                            w_hi, w_lo = wts[:, 2:4, 0, k, :], wts[:, 2:4, 1, k, :]
                        else:
                            o = bank(i)[:, 0:256]
                            w_hi, w_lo = wts[:, 1, 0, k, :], wts[:, 1, 1, k, :]
                        x_hi, x_lo = h[:, 0, k, ts], h[:, 1, k, ts]
                        pe.matmul(o, x_hi, w_hi, start=(k == 0), stop=False)
                        pe.matmul(o, x_hi, w_lo, start=False, stop=False)
                        last = pe.matmul(o, x_lo, w_hi, start=False, stop=(k == KT - 1))
                    last.then_inc(p_main, 1)

            def gate_row():
                pe.wait_ge(d_gdiag, 1)
                pe.wait_ge(a_pt, 2 * NT)
                for half in range(2):
                    last = pe.matmul(tr[:, half, :], ones[:, :], gdiag[:, 4 * half:4 * half + 4, :], start=True, stop=True)
                last.then_inc(p_gbc, 1)

            def ln_mean():
                pe.wait_ge(g_s01, 1)
                pe.wait_ge(d_s23, 1)
                pe.wait_ge(d_cp, 14)
                for half in range(2):
                    sl = slice(half * HALF, (half + 1) * HALF)
                    pe.matmul(ps[:, half, :], ones[:, :], lnA[:, sl], start=True, stop=False)
                    last = pe.matmul(ps[:, half, :], ones[:, :], lnB[:, sl], start=False, stop=True)
                last.then_inc(p_mean, 1)

            def ln_squares():
                pe.wait_ge(a_sq, NCT)
                pe.wait_ge(d_dm, NCT)
                for half in range(2):
                    sl = slice(half * HALF, (half + 1) * HALF)
                    for ct in range(NCT):
                        last = pe.matmul(ps[32 * ct:32 * ct + 32, half, :], ones[:, 0:32], sq[ct][:, sl],
                                         start=True, stop=True)
                last.then_inc(p_sq, 1)

            def ln_var():
                pe.wait_ge(a_lv, 1)
                pe.wait_ge(a_att, NT)
                for t in range(NT):
                    last = pe.matmul(pv[:, t:t + 1], lnA[:, t * P:(t + 1) * P], ones[:, 0:1], start=True, stop=True)
                last.then_inc(p_var, 1)

            for m in range(2 * NCT):
                n = NT + m
                for half in range(2):
                    i = 32 + 2 * m + half
                    for k in range(KT):
                        attention_step(n, half * KT + k)
                        if (m, half, k) == (5, 0, 0):
                            gate_row()
                        if (m, half, k) == (6, 0, 0):
                            ln_mean()
                        if (m, half, k) == (7, 0, 0):
                            ln_squares()
                        if (m, half, k) == (7, 1, 0):
                            ln_var()
                        if k == 0:
                            wait_bank(i)
                        if half == 0 and m % 2 == 0 and k % 4 == 0:
                            pe.wait_ge(g_lo, split_done(7 + m // 2, k // 4))
                        last = channel_step(bank(i), (1 + m // 2) % 3, (m % 2) * P, half, k)
                    last.then_inc(p_main, 1)

            obanks = [tr[:, 0, :], tr[:, 1, :], pm[:, 2, :], pm[:, 0, :], pm[:, 1, :]]

            def out_step(i, k):
                t, n = i % NT, i // NT
                ts = slice(t * P, (t + 1) * P)
                o = obanks[i % 5].rearrange("p (s n) -> p s n", s=2)
                w = [wts[:, (1 - n):4:2, part, k, :] for part in range(2)]
                pe.matmul(o, h[:, 0, k, ts], w[0], start=(k == 0), stop=False)
                pe.matmul(o, h[:, 0, k, ts], w[1], start=False, stop=False)
                return pe.matmul(o, h[:, 1, k, ts], w[0], start=False, stop=(k == KT - 1))

            def wait_y(k, half):
                pe.wait_ge(g_ylo, y_order.index((k, half)) + 1)

            pe.wait_ge(g_lo, split_done(12))
            pe.wait_ge(a_gbc, 1)
            for i in range(5):
                if i >= 2:
                    pe.wait_ge(d_gate, 14 + i - 2)
                for k in range(NCT):
                    if i % 4 == 0:
                        wait_y(k, i // 4)
                    out_step(i, k)
                if i == 1:
                    pe.wait_ge(d_ldiag, 1)
                    for half in range(2):
                        last = pe.matmul(ps[:, half, :], ones[:, :], lnbuf[:, 0, half * HALF:(half + 1) * HALF],
                                         start=True, stop=True)
                    last.then_inc(p_bc, 1)
            for i in range(2 * NT):
                if i >= 5:
                    pe.wait_ge(d_o, i - 4)
                if i == NT:
                    pe.wait_ge(g_lo, split_done(14))
                for k in range(NCT if i < 5 else 0, KT):
                    if i in (0, 4) and k >= NCT:
                        wait_y(k, i // 4)
                    last = out_step(i, k)
                last.then_inc(p_out, 1)

        @block.scalar
        def _(act):
            linked = [0]

            def link(ins):
                linked[0] += 1
                ins.then_inc(a_link, 1)
                act.wait_ge(a_link, linked[0])

            act.wait_ge(p_rows, 1)
            act.activation(cols[:, :], pv[:, 0:52], ACT.Copy).then_inc(a_cols, 1)
            act.wait_ge(a_cols, 1)
            act.activation(cact[:, :], cols[:, C_C:C_C + KT], ACT.Tanh, scale=0.5).then_inc(a_cols, 1)

            def sum_x(t):
                act.wait_ge(s_x[t], 16)
                if t:
                    act.wait_ge(a_ssx, t)
                act.activation(junk[:, :], xs[:, t, :], ACT.Square, accum_out=ssx[:, t:t + 1]).then_inc(a_ssx, 1)

            def w_hi(i):
                u, _ = pieces[i]
                r = raw_at["w", i]
                act.wait_ge(s_raw[r % 3], raw_due[r])
                if free[u]:
                    act.wait_ge(p_main, free[u])
                slot, ks = whalf(i)
                act.activation(wts[:, slot, 0, ks, :], raw[:, r % 3, :].rearrange("p (k n) -> p k n", k=4),
                               ACT.Copy).then_inc(a_hi, 1)

            def modulate(idx):
                k = idx % KT
                act.wait_ge(p_xT, idx + 1)
                if idx < KT:
                    act.wait_ge(d_ab, 2 * k + 2)
                if idx >= 2:
                    act.wait_ge(d_hlo, idx - 1)
                half = idx // KT
                for dst in (h32[:, idx % 2, :], h[:, 0, k, half * HALF:(half + 1) * HALF]):
                    last = act.activation(dst, tr[:, idx % 2, :], ACT.Identity, scale=modA[:, k:k + 1],
                                          bias=modB[:, k:k + 1])
                last.then_inc(a_h32, 1)

            act.wait_ge(g_const, 4)
            sum_x(0)
            sum_x(1)
            sum_x(2)
            sum_x(3)
            act.wait_ge(p_rows, 2)
            act.activation(cw[:, :, :], pv[:, 64:192].rearrange("p (i t) -> p i t", t=32)[:, :, 0:TAPS], ACT.Copy,
                           scale=0.5).then_inc(a_cols, 1)
            for i in range(3):
                w_hi(i)
            modulate(0)
            w_hi(3)
            for k in range(1, KT):
                modulate(k)
                if k == 3:
                    w_hi(4)
                if k == 6:
                    w_hi(5)
                if k >= 4:
                    sum_x(k)

            def tanh_g(i, half, src, use):
                act.wait_ge(p_main, use + 1)
                act.activation(z[:, i, PAD + half * HALF:PAD + (half + 1) * HALF], src, ACT.Tanh,
                               scale=0.5).then_inc(a_tanh, 1)

            tanh_g(0, 0, pm[:, 0, :], 0)
            tanh_g(1, 0, pm[:, 1, :], 1)
            for idx in range(KT, 2 * KT):
                modulate(idx)
                if idx == KT + 2:
                    tanh_g(2, 0, ps[:, 1, :], 4)
            tanh_g(3, 0, pv[:, :], 5)

            def gate_product(i):
                r = raw_at["g", i]
                act.wait_ge(s_raw[r % 3], raw_due[r])
                if i == 0:
                    act.wait_ge(p_xT, 16)
                dst = gacc[:, :] if i == 0 else raw[:, r % 3, :]
                act.activation(dst, raw[:, r % 3, :], ACT.Copy, scale=cact[:, i:i + 1]).then_inc(a_gp, 1)

            for i in range(3):
                gate_product(i)
            tanh_g(0, 1, pm[:, 0, :], 6)
            gate_product(3)
            gate_product(4)
            tanh_g(1, 1, pm[:, 2, :], 8)
            for i in range(5, KT):
                gate_product(i)
            w_hi(6)
            w_hi(7)
            tanh_g(2, 1, pm[:, 0, :], 10)
            w_hi(8)
            w_hi(9)
            tanh_g(3, 1, pm[:, 1, :], 11)
            for i in range(10, 14):
                w_hi(i)

            def bank(i):
                return pm[:, (i - 10) % 3, :]

            def squares_v(t):
                act.wait_ge(p_main, 16 + 2 * t + 2)
                if t:
                    act.wait_ge(g_rope, t)
                    act.wait_ge(d_ss, t)
                if t >= 5:
                    act.wait_ge(p_PV, 2 * (t - 4) + 2)
                act.activation(rot2[:, 0:512], bank(16 + 2 * t), ACT.Square)
                act.activation(rot2[:, 512:640], bank(17 + 2 * t)[:, 0:P], ACT.Square)
                act.activation(qk[:, 0:512], bank(16 + 2 * t), ACT.Copy)
                act.activation(qk[:, 512:640], bank(17 + 2 * t)[:, 0:P], ACT.Copy)
                act.activation(v[:, t % 5, :], bank(17 + 2 * t)[:, P:2 * P], ACT.Copy, scale=0.5).then_inc(a_v, 1)

            def copy_pt(b, g):
                act.wait_ge(p_PT, 2 * b + g + 1)
                if b:
                    act.wait_ge(p_PV, 2 * b + g - 1)
                act.activation(pcur[g][:, :, :], tr[:, g, :].rearrange("p (j n) -> p j n", j=GRP), ACT.Copy).then_inc(a_pt, 1)

            def exps(b, part):
                s = sel1 if b % 2 else sel0
                if part == 0:
                    act.wait_ge(d_nmx, b + 1)
                    if b:
                        act.wait_ge(d_rden, b)
                for i in range(4 * part, 4 * part + 4):
                    act.activation(s[:, i, :], s[:, i, :], ACT.Exp, bias=nmx[:, b % 2, i:i + 1],
                                   accum_out=psum_p[:, i:i + 1])
                if part == 1:
                    act.activation(esink[:, :], sdiff[:, :], ACT.Exp).then_inc(a_exp, 1)

            def copy_qk(b):
                act.wait_ge(p_T, b + 1)
                if b:
                    act.wait_ge(p_S, 2 * b)
                act.activation(qT[:, :, :], tr[:, 0, :].rearrange("p (j n) -> p j n", j=GRP), ACT.Copy)
                act.activation(kT[:, b % 2, :], tr[:, 1, 0:P], ACT.Copy).then_inc(a_qT, 1)

            def copy_scores(b, jj):
                s = sel1 if b % 2 else sel0
                act.wait_ge(p_S, 2 * b + jj + 1)
                if b >= 2 and jj == 0:
                    act.wait_ge(p_PT, 2 * (b - 2) + 2)
                src = ps[:, :, :].rearrange("p g (j s n) -> p (g j) s n", j=2, s=2)[:, :, b % 2, :]
                act.activation(s[:, 4 * jj:4 * jj + 4, :], src, ACT.Copy).then_inc(a_sel, 1)

            def normalize(b):
                s = sel1 if b % 2 else sel0
                act.wait_ge(d_rden, b + 1)
                for i in range(NH):
                    last = act.activation(s[:, i, :], s[:, i, :], ACT.Copy, scale=rden[:, i:i + 1])
                last.then_inc(a_pn, 1)

            def copy_att(b):
                act.wait_ge(p_PV, 2 * b + 2)
                act.activation(att[:, :, b * P:(b + 1) * P], pv[:, :].rearrange("p (j n) -> p j n", j=GRP),
                               ACT.Copy).then_inc(a_att, 1)

            def tanh_gate(m, half):
                i = 32 + 2 * m + half
                act.wait_ge(p_main, i + 1)
                if m < NCT:
                    if m == 0:
                        act.wait_ge(d_gcol, 1)
                    if m == 2:
                        act.wait_ge(p_PV, 16)
                    if m == 3:
                        act.wait_ge(p_PT, 16)
                    dst = gb[:, m, half * HALF:(half + 1) * HALF]
                else:
                    if m > NCT:
                        act.wait_ge(d_ya, 2 * (m - NCT - 1) + half + 1)
                    dst = obuf[:, half, :]
                act.activation(dst, bank(i), ACT.Tanh, scale=0.5).then_inc(a_tanh, 1)

            for n in range(16):
                t, b2, b3, b4 = n - 1, n - 2, n - 3, n - 4
                if 0 <= b4 < NT:
                    copy_pt(b4, 0)
                    copy_pt(b4, 1)
                if n > 8 and n != 11:
                    tanh_gate(n - 9, 1)
                if 0 <= t < NT:
                    squares_v(t)
                if 0 <= b3 < NT:
                    exps(b3, 0)
                if 0 <= b2 < NT:
                    copy_qk(b2)
                if 0 <= b3 < NT:
                    exps(b3, 1)
                if 0 <= b2 < NT:
                    copy_scores(b2, 0)
                if 0 <= b4 < NT:
                    copy_att(b4)
                if n == 11:
                    tanh_gate(2, 0)
                    tanh_gate(2, 1)
                if 0 <= b3 < NT:
                    normalize(b3)
                if 0 <= b2 < NT:
                    copy_scores(b2, 1)
                if n == 14:
                    for ct in range(NCT):
                        act.wait_ge(d_dm, ct + 1)
                        if ct == 2:
                            act.wait_ge(p_mean, 1)
                        act.activation(sq[ct], conv_out[ct], ACT.Square).then_inc(a_sq, 1)
                if n == 15:
                    act.wait_ge(p_sq, 1)
                    act.activation(lnA[:, :].rearrange("p (a n) -> p a n", a=2), ps[:, :, :], ACT.Copy).then_inc(a_lv, 1)
                if 7 <= n < 10:
                    w_hi(2 * n)
                    w_hi(2 * n + 1)
                if n >= 8 and n != 10:
                    tanh_gate(n - 8, 0)
                if n == 10:
                    w_hi(20)
                    w_hi(21)
                if n == 12:
                    w_hi(22)
                    w_hi(23)
                if n == 13:
                    act.wait_ge(p_gbc, 1)
                    act.wait_ge(p_PV, 16)
                    act.activation(gbc[:, :].rearrange("p (a n) -> p a n", a=2), tr[:, :, :], ACT.Copy).then_inc(a_gbc, 1)
                    w_hi(24)
                    w_hi(25)

            def y_hi(i):
                k, half = y_order[i]
                sl = slice(half * HALF, (half + 1) * HALF)
                if i < 8:
                    act.wait_ge(d_ya, 2 * k + half + 1)
                    act.wait_ge(p_main, 47 + half)
                else:
                    act.wait_ge(d_yb, i - 7)
                act.activation(h[:, 0, k, sl], y_src(k, sl), ACT.Copy).then_inc(a_yhi, 1)

            for i in range(4):
                y_hi(i)
            tanh_gate(7, 1)
            for i in range(4, 8):
                y_hi(i)
            for i in range(8):
                ct, sl = i % NCT, slice((i // NCT) * HALF, (i // NCT + 1) * HALF)
                act.wait_ge(d_e, i + 1)
                if i >= 2:
                    act.wait_ge(d_yb, i - 1)
                act.activation(sq[1 + 2 * (i % 2)][:, 0:HALF], conv_out[ct][:, sl], ACT.Tanh, scale=lnc[:, 0, ct:ct + 1],
                               bias=lnc[:, 1, ct:ct + 1]).then_inc(a_ty, 1)
                if i >= 1:
                    y_hi(8 + i - 1)
            y_hi(15)
            for i in range(26, 30):
                w_hi(i)

        @block.vector
        def _(dve):
            linked = [0]

            def link(ins):
                linked[0] += 1
                ins.then_inc(d_link, 1)
                dve.wait_ge(d_link, linked[0])

            dve.wait_ge(a_cols, 2)
            link(dve.scalar_tensor_tensor(out=cact[:, :], in0=cact[:, :], scalar=1.0, in1=cols[:, C_C:C_C + KT],
                                          op0=ALU.add, op1=ALU.mult))
            dve.tensor_scalar(cact[:, :], cact[:, :], 0.5, None, ALU.mult).then_inc(d_cact, 1)
            dve.tensor_scalar(bs1[:, :], cols[:, C_SC:C_SC + KT], 1.0, None, ALU.add)
            for i, (c0, f) in enumerate(((C_LW, 0.5), (C_LB, 0.5), (C_LW, 0.25), (C_LB, 0.25))):
                last = dve.tensor_scalar(lnc[:, i, :], cols[:, c0:c0 + NCT], f, None, ALU.mult)
            last.then_inc(d_cact, 1)

            def normalize_x(t):
                dve.tensor_scalar(xs[:, t, :], xs[:, t, :], rsx[:, t:t + 1], None, ALU.mult).then_inc(d_xn, 1)

            def ada_sums(k):
                if k == 0:
                    dve.wait_ge(d_cact, 2)
                dve.wait_ge(s_slab[k % 3], 32 * (k // 3 + 1))
                if k >= 2:
                    dve.wait_ge(p_ada, k - 1)
                for ct in range(7):
                    acc = ada_acc[:, k % 2, ct % 2, :]
                    src = slab[:, k % 3, ct, :, :].rearrange("p a n -> p (a n)")
                    if ct < 2:
                        ins = dve.tensor_scalar(acc, src, cact[:, ct:ct + 1], None, ALU.mult)
                    else:
                        dve.wait_ge(d_ada, 8 * k + ct - 1)
                        ins = dve.scalar_tensor_tensor(out=acc, in0=src, scalar=cact[:, ct:ct + 1], in1=acc,
                                                       op0=ALU.mult, op1=ALU.add)
                    ins.then_inc(d_ada, 1)
                dve.wait_ge(d_ada, 8 * k + 7)
                dve.tensor_tensor(ada_acc[:, k % 2, 0, :], ada_acc[:, k % 2, 0, :], ada_acc[:, k % 2, 1, :],
                                  ALU.add).then_inc(d_ada, 1)

            def ada_finish(k):
                dve.wait_ge(p_ada, k + 1)
                b = pv if k % 2 == 0 else ps[:, 1, :]
                dve.scalar_tensor_tensor(out=modA[:, k:k + 1], in0=b[:, 1:2], scalar=bs1[:, k:k + 1],
                                         in1=cols[:, C_NW + k:C_NW + k + 1], op0=ALU.add, op1=ALU.mult).then_inc(d_ab, 1)
                dve.tensor_tensor(modB[:, k:k + 1], b[:, 0:1], cols[:, C_SH + k:C_SH + k + 1], ALU.add).then_inc(d_ab, 1)

            def split_h(idx):
                half, k = idx // KT, idx % KT
                sl = slice(half * HALF, (half + 1) * HALF)
                dve.wait_ge(a_h32, idx + 1)
                dve.tensor_tensor(h[:, 1, k, sl], h32[:, idx % 2, :], h[:, 0, k, sl].bitcast(F32),
                                  ALU.subtract).then_inc(d_hlo, 1)

            dve.wait_ge(g_rsx, 1)
            for t in range(4):
                normalize_x(t)
            ada_sums(0)
            ada_sums(1)
            ada_finish(0)
            for k in range(KT):
                split_h(k)
                if k + 1 < KT:
                    ada_finish(k + 1)
                if k + 2 < KT:
                    ada_sums(k + 2)
            dve.wait_ge(g_rsx, 2)
            for t in range(4, NT):
                normalize_x(t)
            for idx in range(KT, 2 * KT):
                split_h(idx)
            dve.wait_ge(p_ada, KT)
            dve.memset(z[:, :, 0:PAD], 0.0).then_inc(d_link, 1)
            linked[0] += 1

            def glu(i, half, src, use, n_tanh):
                dve.wait_ge(p_main, use + 1)
                dve.wait_ge(a_tanh, n_tanh)
                sl = slice(PAD + half * HALF, PAD + (half + 1) * HALF)
                dve.scalar_tensor_tensor(out=z[:, i, sl], in0=z[:, i, sl], scalar=1.0, in1=src,
                                         op0=ALU.add, op1=ALU.mult).then_inc(d_glu, 1)

            done = [0, 0]
            tap_value = {}

            def taps(n):
                for step in tap_steps[done[0]:done[0] + n]:
                    for i, j in step:
                        acc = cacc[:, i, :] if i < 2 else z[:, i - 2, 0:S]
                        src = z[:, i, j:j + S]
                        if j == 0:
                            dve.wait_ge(d_link, pads)
                            dve.wait_ge(d_glu, (3, 4, 6, 8)[i])
                            if i >= 2:
                                dve.wait_ge(d_conv, tap_value[i - 2])
                            ins = dve.tensor_scalar(acc, src, cw[:, i, 0:1], cols[:, C_CB + i:C_CB + i + 1],
                                                    ALU.mult, ALU.add)
                        else:
                            dve.wait_ge(d_conv, tap_value[i])
                            ins = dve.scalar_tensor_tensor(out=acc, in0=src, scalar=cw[:, i, j:j + 1], in1=acc,
                                                           op0=ALU.mult, op1=ALU.add)
                        ins.then_inc(d_conv, 1)
                        done[1] += 1
                        tap_value[i] = done[1]
                done[0] += n

            pads = linked[0]
            dve.wait_ge(a_cols, 3)
            glu(0, 0, pm[:, 2, :], 2, 1)
            glu(1, 0, ps[:, 0, :], 3, 2)
            glu(0, 1, pm[:, 1, :], 7, 5)
            taps(6)
            glu(1, 1, ps[:, 0, :], 9, 6)
            taps(6)
            glu(2, 0, pm[:, 2, :], 12, 3)
            taps(2)
            glu(2, 1, pm[:, 0, :], 13, 7)
            taps(2)
            glu(3, 0, pm[:, 1, :], 14, 4)
            taps(2)
            glu(3, 1, pm[:, 2, :], 15, 8)
            taps(1)
            dve.wait_ge(p_gcol, 1)
            dve.tensor_tensor(gcol[:, :], tr[:, 0, 0:KT], cols[:, C_GT:C_GT + KT], ALU.add).then_inc(d_gcol, 1)

            def bank(i):
                return pm[:, (i - 10) % 3, :]

            def sum_squares(t):
                dve.wait_ge(a_v, t + 1)
                if t:
                    dve.wait_ge(g_rs, t)
                dve.tensor_reduce(ssq[:, :], rot2[:, :].rearrange("p (h d) -> p h d", d=DH), AX.X, ALU.add).then_inc(d_ss, 1)

            def normalize_qk(t):
                dve.wait_ge(g_rs, t + 1)
                heads = qk[:, :].rearrange("p (h d) -> p h d", d=DH)
                dve.tensor_tensor(heads, heads, rsq[:, :].unsqueeze(2).to_broadcast([P, NH + NKV, DH]),
                                  ALU.mult).then_inc(d_qn, 1)

            def previous_keys(b, jj):
                s = sel1 if b % 2 else sel0
                dve.wait_ge(a_sel, 2 * b + jj + 1)
                src = ps[:, :, :].rearrange("p g (j s n) -> p (g j) s n", j=2, s=2)[:, :, 1 - b % 2, :]
                dve.copy_predicated(s[:, 4 * jj:4 * jj + 4, :], later[:, :].unsqueeze(1).to_broadcast([P, 4, P]),
                                    src).then_inc(d_cp, 1)

            def row_max(b):
                s = sel1 if b % 2 else sel0
                if b == 0:
                    dve.wait_ge(g_blk0, 1)
                else:
                    dve.wait_ge(d_cp, 2 * b)
                if b:
                    dve.wait_ge(a_exp, b)
                link(dve.tensor_reduce(nmx[:, b % 2, :], s[:, :, :], AX.X, ALU.max, negate=True))
                m = nmx[:, b % 2, :].rearrange("p (jj g jh) -> p jj g jh", jj=2, g=NKV)
                link(dve.tensor_tensor(m, m, nsnk[:, :].rearrange("p (g jj jh) -> p jj g jh", g=NKV, jj=2), ALU.min))
                dve.tensor_tensor(sdiff[:, :].rearrange("p (jj g jh) -> p jj g jh", jj=2, g=NKV), m,
                                  snk[:, :].rearrange("p (g jj jh) -> p jj g jh", g=NKV, jj=2), ALU.add).then_inc(d_nmx, 1)

            def denominators(b):
                dve.wait_ge(a_exp, b + 1)
                if b:
                    dve.wait_ge(a_pn, b)
                link(dve.tensor_tensor(psum_p[:, :], psum_p[:, :], esink[:, :], ALU.add))
                dve.reciprocal(rden[:, :], psum_p[:, :]).then_inc(d_rden, 1)

            def gate(m, half):
                i = 32 + 2 * m + half
                sl = slice(half * HALF, (half + 1) * HALF)
                dve.wait_ge(a_tanh, 8 + 2 * m + half + 1)
                dst = gb[:, m, sl] if m < NCT else obuf[:, half, :]
                dve.scalar_tensor_tensor(out=dst, in0=dst, scalar=1.0, in1=bank(i), op0=ALU.add,
                                         op1=ALU.mult).then_inc(d_gate, 1)
                if m >= NCT:
                    j = m - NCT
                    dve.wait_ge(d_gate, 2 * m + half + 1)
                    dve.wait_ge(a_att, NT)
                    dve.tensor_tensor(att[:, j, sl], att[:, j, sl], obuf[:, half, :], ALU.mult).then_inc(d_ya, 1)

            def s23():
                dve.wait_ge(d_conv, 4 * TAPS)
                dve.wait_ge(p_PV, 16)
                dve.tensor_tensor(lnB[:, :], conv_out[2], conv_out[3], ALU.add).then_inc(d_s23, 1)

            def minus_mean():
                dve.wait_ge(p_mean, 1)
                for ct in range(NCT):
                    dve.scalar_tensor_tensor(out=conv_out[ct], in0=ps[:, :, :].rearrange("p a n -> p (a n)"),
                                             scalar=-1.0 / 512, in1=conv_out[ct], op0=ALU.mult,
                                             op1=ALU.add).then_inc(d_dm, 1)

            def variances():
                dve.wait_ge(p_var, 1)
                dve.tensor_copy(ssx[:, :], pv[:, 0:NT]).then_inc(d_var, 1)
                dve.wait_ge(g_rstd, 1)
                dve.tensor_tensor(lnbuf[:, 0, 0:S].rearrange("p (t n) -> p t n", t=NT),
                                  ident[:, :].unsqueeze(1).to_broadcast([P, NT, P]),
                                  rsx[:, :].unsqueeze(2).to_broadcast([P, NT, P]), ALU.mult).then_inc(d_ldiag, 1)

            for n in range(16):
                t, b2, b3 = n - 1, n - 2, n - 3
                if n == 0:
                    taps(3)
                if n == 11:
                    gate(2, 0)
                if n > 8:
                    gate(n - 9, 1)
                if 0 <= t < NT:
                    if t > 1:
                        taps(1)
                    sum_squares(t)
                    taps(1)
                    normalize_qk(t)
                taps(1)
                if 0 <= b3 < NT:
                    denominators(b3)
                if 0 <= b2 < NT:
                    if b2:
                        previous_keys(b2, 0)
                    taps(1)
                    if b2:
                        previous_keys(b2, 1)
                    row_max(b2)
                if n >= 10:
                    taps(2)
                if n == 12:
                    dve.wait_ge(p_PT, 16)
                    dve.wait_ge(g_rope, NT)
                    dve.wait_ge(p_T, NT)
                    dve.tensor_tensor(gdiag[:, :, :], ident[:, :].unsqueeze(1).to_broadcast([P, KT, P]),
                                      gcol[:, :].unsqueeze(2).to_broadcast([P, KT, P]), ALU.mult).then_inc(d_gdiag, 1)
                if n == 14:
                    minus_mean()
                if n >= 8 and n != 10:
                    gate(n - 8, 0)
                if n == 13:
                    taps(len(tap_steps) - done[0])
                    s23()
            variances()
            gate(7, 1)
            dve.wait_ge(p_bc, 1)

            def normed(i):
                e, sl = conv_out[i % NCT], slice((i // NCT) * HALF, (i // NCT + 1) * HALF)
                dve.tensor_tensor(e[:, sl], e[:, sl], ps[:, i // NCT, :], ALU.mult).then_inc(d_e, 1)

            normed(0)
            for i in range(8):
                ct, sl = i % NCT, slice((i // NCT) * HALF, (i // NCT + 1) * HALF)
                if i < 7:
                    normed(i + 1)
                e, ty = conv_out[ct][:, sl], sq[1 + 2 * (i % 2)][:, 0:HALF]
                dve.wait_ge(a_ty, i + 1)
                link(dve.tensor_scalar(e, e, lnc[:, 2, ct:ct + 1], lnc[:, 3, ct:ct + 1], ALU.mult, ALU.add))
                link(dve.scalar_tensor_tensor(out=ty, in0=ty, scalar=1.0, in1=e, op0=ALU.add, op1=ALU.mult))
                dve.tensor_tensor(gb[:, ct, sl], gb[:, ct, sl], ty, ALU.mult).then_inc(d_yb, 1)

            obanks = [tr[:, 0, :], tr[:, 1, :], pm[:, 2, :], pm[:, 0, :], pm[:, 1, :]]
            for i in range(2 * NT):
                n = i // NT
                dve.wait_ge(p_out, i + 1)
                if i >= 2:
                    dve.wait_ge(g_fin, i - 1)
                dve.tensor_tensor(obuf[:, i % 2, :], obanks[i % 5], gbc[:, n * HALF:(n + 1) * HALF],
                                  ALU.mult).then_inc(d_o, 1)


def rope_table():
    inv = (10000.0 ** (-np.arange(0, DH, 2) / DH)).astype(np.float32)
    ang = np.arange(S, dtype=np.float32)[:, None] * inv[None, :]
    co, si = np.cos(ang), np.sin(ang)
    return np.ascontiguousarray(np.concatenate([co, co, -si, si], axis=1).astype(np.float32))


_INS = ["x", "c", "w_ada", "b_ada", "norm_w", "w_in", "q_norm_w", "k_norm_w", "sinks", "conv_w", "conv_b",
        "ln_w", "ln_b", "w_out"]


def kernel(**inputs):
    import concourse.bacc as bacc
    from concourse.bass_utils import run_bass_kernel_spmd

    nc = bacc.Bacc("TRN2", target_bir_lowering=False, num_devices=1)
    arrays = {f"in_{n}": np.ascontiguousarray(inputs[n]) for n in _INS}
    arrays["in_rope"] = rope_table()
    args = [nc.dram_tensor(n, a.shape, mybir.dt.from_np(a.dtype), kind="ExternalInput").ap() for n, a in arrays.items()]
    args.append(nc.dram_tensor("out_0", (1, S, D), F32, kind="ExternalOutput").ap())
    build(nc, *args)
    return run_bass_kernel_spmd(nc, [arrays], core_ids=[0]).results[0]["out_0"]
```
